# Optimizing a Trainium2 kernel written in Bass

```python
import jax, jax.numpy as jnp
from jax import lax
import numpy as np

D_MODEL = 1024
BATCH = 1
SEQ = 512
DEPTH = 2

EPS = 1e-6
HEAD_DIM = 64
MIX_WIDTH = D_MODEL
N_GROUPS = 4
GROUP_WIDTH = MIX_WIDTH // N_GROUPS
POOL_WINDOWS = (2, 4, 8, 16)
POOL_GROUP = GROUP_WIDTH // len(POOL_WINDOWS)
SWA_Q_HEADS = GROUP_WIDTH // HEAD_DIM
SWA_KV_HEADS = 2
SWA_GQA = SWA_Q_HEADS // SWA_KV_HEADS
SWA_WINDOW = 128
SWA_BLOCK = SWA_WINDOW
CONV_WIDTH = 3
DIFF_HEADS = GROUP_WIDTH // HEAD_DIM
DIFF_QK_DIM = HEAD_DIM // 2
DIFF_V_DIM = HEAD_DIM
Q_BLOCK = 128
SPLITS = (GROUP_WIDTH,
          SWA_Q_HEADS * HEAD_DIM, SWA_KV_HEADS * HEAD_DIM, SWA_KV_HEADS * HEAD_DIM,
          GROUP_WIDTH, GROUP_WIDTH, GROUP_WIDTH,
          DIFF_HEADS * 2 * DIFF_QK_DIM, DIFF_HEADS * 2 * DIFF_QK_DIM, DIFF_HEADS * DIFF_V_DIM)
IN_PROJ_WIDTH = sum(SPLITS)
PEER_HEADS = 8
PEER_KEYS = 128
PEER_EXPERTS = PEER_KEYS * PEER_KEYS
PEER_QUERY_DIM = 256
PEER_HALF = PEER_QUERY_DIM // 2
PEER_TOPK = 16
PEER_TOKEN_BLOCK = 128

kernel_name = "hymba_pool_swa_conv_diff_peer"

def rms_norm(x, g):
    xf = x.astype(jnp.float32)
    y = xf * lax.rsqrt(jnp.mean(xf * xf, axis=-1, keepdims=True) + EPS)
    return (y * g.astype(jnp.float32)).astype(x.dtype)

def head_norm(y, g):
    b, s, w = y.shape
    nh = w // HEAD_DIM
    return rms_norm(y.reshape(b, s, nh, HEAD_DIM), g.reshape(nh, HEAD_DIM)).reshape(b, s, w)

def split_cols(z, sizes):
    out, off = [], 0
    for n in sizes:
        out.append(z[..., off:off + n])
        off += n
    return out

def alibi_slopes(n):
    return jnp.exp2(-8.0 * jnp.arange(1, n + 1, dtype=jnp.float32) / n)

def pool_mixer(p, w_pool):
    b, s, _ = p.shape
    pf = p.astype(jnp.float32).reshape(b, s, len(POOL_WINDOWS), POOL_GROUP)
    cs = jnp.cumsum(pf, axis=1)
    t = jnp.arange(s)
    pooled = []
    for gi, w in enumerate(POOL_WINDOWS):
        c = cs[:, :, gi]
        lagged = jnp.pad(c, ((0, 0), (w, 0), (0, 0)))[:, :s]
        cnt = jnp.minimum(t + 1, w).astype(jnp.float32)[None, :, None]
        pooled.append((c - lagged) / cnt)
    d = (jnp.stack(pooled, axis=2) - pf).astype(p.dtype)
    return jnp.einsum('bsgc,gcd->bsgd', d, w_pool).reshape(b, s, GROUP_WIDTH)

def swa_sink_attention(q, k, v, qn_g, kn_g, sinks, slopes):
    b, s, _ = q.shape
    nb = s // SWA_BLOCK
    q = rms_norm(q.reshape(b, s, SWA_KV_HEADS, SWA_GQA, HEAD_DIM), qn_g)
    k = rms_norm(k.reshape(b, s, SWA_KV_HEADS, HEAD_DIM), kn_g)
    v = v.reshape(b, s, SWA_KV_HEADS, HEAD_DIM)
    qb = q.reshape(b, nb, SWA_BLOCK, SWA_KV_HEADS, SWA_GQA, HEAD_DIM)

    def banded(a):
        ap = jnp.pad(a, ((0, 0), (SWA_BLOCK, 0), (0, 0), (0, 0)))
        blk = ap.reshape(b, nb + 1, SWA_BLOCK, SWA_KV_HEADS, HEAD_DIM)
        return jnp.concatenate([blk[:, :-1], blk[:, 1:]], axis=2)

    kb, vb = banded(k), banded(v)
    sc = jnp.einsum('bnqhgd,bnkhd->bhgnqk', qb, kb).astype(jnp.float32) * (HEAD_DIM ** -0.5)
    i = jnp.arange(SWA_BLOCK)[:, None]
    j = jnp.arange(2 * SWA_BLOCK)[None, :]
    dist = i + SWA_BLOCK - j
    kpos = jnp.arange(nb)[:, None, None] * SWA_BLOCK - SWA_BLOCK + j
    valid = (dist >= 0) & (dist < SWA_WINDOW) & (kpos >= 0)
    m_h = slopes.reshape(SWA_KV_HEADS, SWA_GQA)[None, :, :, None, None, None]
    sc = sc - m_h * dist.astype(jnp.float32)
    sc = jnp.where(valid[None, None, None], sc, -jnp.inf)
    sink = sinks.astype(jnp.float32).reshape(SWA_KV_HEADS, SWA_GQA)[None, :, :, None, None, None]
    mx = jnp.maximum(jnp.max(sc, axis=-1, keepdims=True), sink)
    e = jnp.exp(sc - mx)
    pr = e / (jnp.sum(e, axis=-1, keepdims=True) + jnp.exp(sink - mx))
    o = jnp.einsum('bhgnqk,bnkhd->bnqhgd', pr.astype(v.dtype), vb)
    return o.reshape(b, s, SWA_Q_HEADS * HEAD_DIM)

def short_conv_mixer(h, gate_b, gate_c, conv_w):
    z = gate_c * h
    y = lax.conv_general_dilated(z, conv_w[:, None, :].astype(z.dtype), window_strides=(1,),
                                 padding=[(CONV_WIDTH - 1, 0)],
                                 dimension_numbers=('NWC', 'WIO', 'NWC'),
                                 feature_group_count=GROUP_WIDTH)
    return gate_b * y

def diff_attention(q, k, v, qn_g, kn_g, lam, slopes):
    b, s, _ = q.shape
    nb = s // Q_BLOCK
    q = rms_norm(q.reshape(b, s, DIFF_HEADS, 2, DIFF_QK_DIM), qn_g)
    k = rms_norm(k.reshape(b, s, DIFF_HEADS, 2, DIFF_QK_DIM), kn_g)
    v = v.reshape(b, s, DIFF_HEADS, DIFF_V_DIM)
    qb = jnp.moveaxis(q.reshape(b, nb, Q_BLOCK, DIFF_HEADS, 2, DIFF_QK_DIM), 1, 0)
    kpos = jnp.arange(s)
    m_h = slopes[None, :, None, None, None]

    def block(args):
        qi, n = args
        qpos = n * Q_BLOCK + jnp.arange(Q_BLOCK)
        sc = jnp.einsum('bqhmd,bkhmd->bhmqk', qi, k).astype(jnp.float32) * (DIFF_QK_DIM ** -0.5)
        dist = qpos[:, None] - kpos[None, :]
        sc = sc - m_h * dist.astype(jnp.float32)
        sc = jnp.where(dist >= 0, sc, -jnp.inf)
        a = jax.nn.softmax(sc, axis=-1)
        w = a[:, :, 0] - lam * a[:, :, 1]
        return jnp.einsum('bhqk,bkhd->bqhd', w.astype(v.dtype), v)

    o = lax.map(block, (qb, jnp.arange(nb)))
    return jnp.moveaxis(o, 0, 1).reshape(b, s, DIFF_HEADS * DIFF_V_DIM)

def peer_ffn(xn, w_query, sub_keys, peer_u, peer_v):
    b, s, d = xn.shape
    t = b * s
    xt = xn.reshape(t, d)
    q = (xt @ w_query).reshape(t, PEER_HEADS, 2, PEER_HALF)
    sk = jnp.einsum('thcd,ckd->thck', q, sub_keys).astype(jnp.float32)
    top_s, top_i = lax.top_k(sk, PEER_TOPK)
    cand_s = top_s[:, :, 0, :, None] + top_s[:, :, 1, None, :]
    cand_i = top_i[:, :, 0, :, None] * PEER_KEYS + top_i[:, :, 1, None, :]
    cand_s = cand_s.reshape(t, PEER_HEADS, PEER_TOPK * PEER_TOPK)
    cand_i = cand_i.reshape(t, PEER_HEADS, PEER_TOPK * PEER_TOPK)
    best_s, best_pos = lax.top_k(cand_s, PEER_TOPK)
    idx = jnp.take_along_axis(cand_i, best_pos, axis=-1)
    gate = jax.nn.softmax(best_s, axis=-1)
    nblk = t // PEER_TOKEN_BLOCK

    def block(args):
        xb, ib, gb = args
        h = jnp.einsum('thkd,td->thk', peer_u[ib], xb).astype(jnp.float32)
        a = (gb * jax.nn.gelu(h, approximate=False)).astype(xb.dtype)
        return jnp.einsum('thk,thkd->td', a, peer_v[ib])

    out = lax.map(block, (xt.reshape(nblk, PEER_TOKEN_BLOCK, d),
                          idx.reshape(nblk, PEER_TOKEN_BLOCK, PEER_HEADS, PEER_TOPK),
                          gate.reshape(nblk, PEER_TOKEN_BLOCK, PEER_HEADS, PEER_TOPK)))
    return out.reshape(b, s, d).astype(xn.dtype)

def hybrid_layer(x, layer_idx, norm1_g, w_in, w_pool, swa_q_norm, swa_k_norm, swa_sinks, conv_w,
                 diff_q_norm, diff_k_norm, lam_q1, lam_k1, lam_q2, lam_k2, out_norm_g, w_out,
                 norm2_g, w_query, sub_keys, peer_u, peer_v):
    slopes = alibi_slopes(SWA_Q_HEADS + DIFF_HEADS)
    lam_init = 0.8 - 0.6 * float(np.exp(-0.3 * layer_idx))
    lam = (jnp.exp(jnp.sum(lam_q1.astype(jnp.float32) * lam_k1.astype(jnp.float32)))
           - jnp.exp(jnp.sum(lam_q2.astype(jnp.float32) * lam_k2.astype(jnp.float32))) + lam_init)

    xn = rms_norm(x, norm1_g)
    z = xn @ w_in
    p_a, q_b, k_b, v_b, h_c, b_c, c_c, q_d, k_d, v_d = split_cols(z, SPLITS)

    y_a = pool_mixer(p_a, w_pool)
    y_b = swa_sink_attention(q_b, k_b, v_b, swa_q_norm, swa_k_norm, swa_sinks, slopes[:SWA_Q_HEADS])
    y_c = short_conv_mixer(h_c, b_c, c_c, conv_w)
    y_d = diff_attention(q_d, k_d, v_d, diff_q_norm, diff_k_norm, lam, slopes[SWA_Q_HEADS:])

    g_a, g_b, g_c, g_d = split_cols(out_norm_g, (GROUP_WIDTH,) * N_GROUPS)
    y = jnp.concatenate([head_norm(y_a, g_a), head_norm(y_b, g_b), head_norm(y_c, g_c),
                         head_norm(y_d, g_d) * (1.0 - lam_init)], axis=-1)
    x = x + y @ w_out
    x = x + peer_ffn(rms_norm(x, norm2_g), w_query, sub_keys, peer_u, peer_v)
    return x

def setup_inputs(seed: int = 0) -> dict:
    key = jax.random.key(seed)
    ks = jax.random.split(key, 24)
    nrm = lambda k, shape, scale: jax.random.normal(k, shape, jnp.float32) * scale
    gain = lambda k, shape: 1.0 + 0.02 * jax.random.normal(k, shape, jnp.float32)
    L = DEPTH
    return {
        "x": nrm(ks[0], (BATCH, SEQ, D_MODEL), 1.0),
        "norm1_g": gain(ks[1], (L, D_MODEL)),
        "w_in": nrm(ks[2], (L, D_MODEL, IN_PROJ_WIDTH), D_MODEL ** -0.5),
        "w_pool": nrm(ks[3], (L, len(POOL_WINDOWS), POOL_GROUP, POOL_GROUP), POOL_GROUP ** -0.5),
        "swa_q_norm": gain(ks[4], (L, HEAD_DIM)),
        "swa_k_norm": gain(ks[5], (L, HEAD_DIM)),
        "swa_sinks": nrm(ks[6], (L, SWA_Q_HEADS), 1.0),
        "conv_w": nrm(ks[7], (L, CONV_WIDTH, GROUP_WIDTH), CONV_WIDTH ** -0.5),
        "diff_q_norm": gain(ks[8], (L, DIFF_QK_DIM)),
        "diff_k_norm": gain(ks[9], (L, DIFF_QK_DIM)),
        "lam_q1": nrm(ks[10], (L, DIFF_QK_DIM), 0.1),
        "lam_k1": nrm(ks[11], (L, DIFF_QK_DIM), 0.1),
        "lam_q2": nrm(ks[12], (L, DIFF_QK_DIM), 0.1),
        "lam_k2": nrm(ks[13], (L, DIFF_QK_DIM), 0.1),
        "out_norm_g": gain(ks[14], (L, MIX_WIDTH)),
        "w_out": nrm(ks[15], (L, MIX_WIDTH, D_MODEL), MIX_WIDTH ** -0.5),
        "norm2_g": gain(ks[16], (L, D_MODEL)),
        "w_query": nrm(ks[17], (L, D_MODEL, PEER_HEADS * PEER_QUERY_DIM), D_MODEL ** -0.5),
        "sub_keys": nrm(ks[18], (L, 2, PEER_KEYS, PEER_HALF), PEER_HALF ** -0.5),
        "peer_u": nrm(ks[19], (L, PEER_EXPERTS, D_MODEL), D_MODEL ** -0.5),
        "peer_v": nrm(ks[20], (L, PEER_EXPERTS, D_MODEL), PEER_HEADS ** -0.5),
    }

def reference(x, norm1_g, w_in, w_pool, swa_q_norm, swa_k_norm, swa_sinks, conv_w, diff_q_norm,
              diff_k_norm, lam_q1, lam_k1, lam_q2, lam_k2, out_norm_g, w_out, norm2_g, w_query,
              sub_keys, peer_u, peer_v):
    for l in range(DEPTH):
        x = hybrid_layer(x, l, norm1_g[l], w_in[l], w_pool[l], swa_q_norm[l], swa_k_norm[l],
                         swa_sinks[l], conv_w[l], diff_q_norm[l], diff_k_norm[l], lam_q1[l],
                         lam_k1[l], lam_q2[l], lam_k2[l], out_norm_g[l], w_out[l], norm2_g[l],
                         w_query[l], sub_keys[l], peer_u[l], peer_v[l])
    return x


_drawn_inputs = setup_inputs


def setup_inputs(seed=0):
    import zlib

    import numpy as np

    out = dict(_drawn_inputs(seed))
    spreads = {}
    factors = {'swa_q_norm': 2.946,
     'swa_k_norm': 2.768,
     'swa_sinks': 8.0,
     'diff_q_norm': 2.854,
     'diff_k_norm': 2.723}
    for name, (base, spread) in spreads.items():
        noise = np.random.default_rng([zlib.crc32(name.encode()), seed]).standard_normal(out[name].shape)
        drawn = base * np.exp(spread * noise) if base else spread * noise
        out[name] = __import__('jax').numpy.asarray(drawn.astype(out[name].dtype))
    for name, factor in factors.items():
        out[name] = (out[name] * factor).astype(out[name].dtype)
    return out
```

```python
import math
from contextlib import ExitStack

import numpy as np
import concourse.bass as bass
from concourse import mybir

DEPTH, SEQ, DM = 2, 512, 1024
P = 128
HALF = 256
TT = HALF // P
NBLK = 2 * DEPTH
KD = DM // P
EPS = 1e-6
PAD = 16
HEADS, TOPK, NKEYS = 8, 16, 128
NEXP = NKEYS * NKEYS
CH = 4
CHUNKS = HEADS * TT * TOPK // CH
SLOTS = 8
NDIAG = 4
WS = 4
BIG = 3.0e38
MASK = -1.0e30

ZQB, ZKB, ZQD, ZKD = (0, 1), 2, (3, 4), (5, 6)
NORMED = 7
ZP, ZH, ZG, ZC = (7, 8), (9, 10), (11, 12), (13, 14)
NZ = 15
NV = 3
WBLOCKS = NZ + NV + 8 + 16
ITEMS = 16
YORDER = (4, 5, 2, 3, 0, 1, 6, 7)

SP_G1, SP_G2, SP_OG, SP_QKG, SP_CONV, SP_SINK, SP_LAM = 0, 8, 16, 24, 31, 37, 41
SP_N = SP_LAM + 128
CC_ID, CC_O64, CC_O32, CC_DB, CC_DD, CC_IOTA, CC_INVW, CC_CORR, CC_SLI, CC_EPS = (
    0, 128, 256, 384, 640, 1152, 1168, 1170, 1202, 1206)
CC_N = CC_EPS + 1


def slope(h):
    return 2.0 ** -(h + 1)


def lam_init(layer):
    return 0.8 - 0.6 * float(np.exp(-0.3 * layer))


def layout_jobs():
    jobs = [(("xT", t, h), "dve", None) for t in range(TT) for h in range(2)]
    jobs += [(("z", i), "act", i) for i in range(NORMED)]
    jobs += [(("v", i), "act", NORMED + i) for i in range(NV)]
    for i in range(NORMED, NZ):
        jobs.append((("z", i), "act", NV + i))
        if i > NORMED:
            jobs.append((("n", i - NORMED - 1), "act", None))
    scores = lambda a: [(("s", a, k), "dve", None) for k in range(1 if a < 8 else 2)]
    jobs += scores(0) + scores(1)
    for a in range(ITEMS + 1):
        if a < ITEMS:
            jobs.append((("t", a), "act", None))
            if a + 2 < ITEMS:
                jobs += scores(a + 2)
        if a:
            jobs.append((("o", a - 1), "act", None))
    jobs += [(("pool", j), "act", None) for j in range(2)]
    jobs += [(("y", i), "act", None) for i in range(8)]
    jobs += [(("out", i), "dve", NZ + NV + i) for i in range(8)]
    jobs += [(("x2T", t, h), "dve", None) for t in range(TT) for h in range(2)]
    jobs += [(("q", i), "act", NZ + NV + 8 + i) for i in range(16)]
    jobs += [(("sk", t, g), "act", None) for t in range(TT) for g in range(4)]
    return jobs


JOBS = layout_jobs()
NJOBS = len(JOBS)
JOB_AT = {name: n for n, (name, _, _) in enumerate(JOBS)}
JOB_BY = {name: by for name, by, _ in JOBS}
JOBS_OF = {by: sum(b == by for _, b, _ in JOBS) for by in ("act", "dve")}
JOB_NTH = {name: sum(b == by for _, b, _ in JOBS[:n + 1]) for n, (name, by, _) in enumerate(JOBS)}
W_JOB = {w: name for name, _, w in JOBS if w is not None}
BANKS = 6


def item(a, t0):
    swa = a < 8
    t, h = t0 + a % 8 // 4, a % 4
    return swa, t, h, (max(t - 1, 0) if swa else 0)


def build(nc, x_d, wall_d, small_d, consts_d, g2b_d, wpool_d, skt_d, uv_d, out_d):
    f32, u32 = mybir.dt.float32, mybir.dt.uint32
    ALU, ACT, AX = mybir.AluOpType, mybir.ActivationFunctionType, mybir.AxisListType.X
    ctx = ExitStack()
    with ctx:
        def sb(name, *shape, dt=f32):
            return ctx.enter_context(nc.sbuf_tensor(name, [P, *shape], dt))

        def sem(name):
            return ctx.enter_context(nc.semaphore(name))

        x = sb("x", SEQ // P, DM)
        gather = sb("gather", SLOTS, 2 * DM)
        xnT = sb("xnT", KD, HALF)
        shared = sb("shared", 16 * HALF + 512)
        zt = shared[:, 0:10 * HALF].rearrange("p (i t) -> p i t", t=HALF)
        sc = shared[:, 10 * HALF:10 * HALF + 2048].rearrange("p (s m k) -> p s m k", s=2, m=2)
        pool_sum = shared[:, 10 * HALF:10 * HALF + 4 * (PAD + HALF)].rearrange("p (i t) -> p i t", i=4)
        qT = shared[:, 0:16 * HALF].rearrange("p (i t) -> p i t", t=HALF)
        kB = sb("kB", SEQ)
        kD = sb("kD", 2, SEQ)
        vAll = sb("vAll", SEQ // P, NV * P)
        pT = sb("pT", 2, PAD + SEQ)
        cT = sb("cT", 2, PAD + SEQ)
        pd = sb("pd", 2, HALF)
        yT = sb("yT", 8, HALF)
        xn = yT[:, :, :].rearrange("p i t -> p (i t)").rearrange("p (t d) -> p t d", t=TT)
        scores = sb("scores", TT, 16, NKEYS)
        w = sb("w", WS, KD, P)
        small = sb("small", DEPTH, SP_N)
        cc = sb("cc", CC_N)
        g2b = sb("g2b", DEPTH, DM)
        wpool = sb("wpool", DEPTH, 2, P)
        skt = sb("skt", DEPTH, 2, NKEYS)
        sq = sb("sq", 2, HALF)
        sd = sb("sd", 2, HALF)
        pt = sb("pt", 2, 512)
        ss = sb("ss", 4)
        sdv = sb("sdv", 4)
        r1 = sb("r1", TT)
        r2 = sb("r2", SEQ // P)
        st = sb("st", 2, 12)
        lam_t = sb("lam_t", DEPTH, 2, 32)
        lam_s = sb("lam_s", DEPTH, 2)
        lam_e = sb("lam_e", DEPTH, 2)
        neg_lam = sb("neg_lam", DEPTH)
        xc = sb("xc", DM)
        top_v = sb("top_v", 2, TOPK)
        top_i = sb("top_i", 2, TOPK, dt=u32)
        top_f = sb("top_f", 2, TOPK)
        sc2 = sb("sc2", 2, NKEYS)
        cand = sb("cand", TOPK, TOPK)
        cand2 = sb("cand2", TOPK, TOPK)
        best_v = sb("best_v", TOPK)
        best_p = sb("best_p", TOPK, dt=u32)
        pos_u = sb("pos_u", 2, TOPK, dt=u32)
        pos_f = sb("pos_f", 2, TOPK)
        hot = sb("hot", 2 * TOPK, TOPK)
        ij = sb("ij", 2, TOPK)
        idx = sb("idx", 2, TOPK, dt=u32)
        neg_best = sb("neg_best", 1)
        gate_e = sb("gate_e", TOPK)
        gate_s = sb("gate_s", 2)
        gate = sb("gate", 2, TOPK)
        hdot = sb("hdot", 2, CH)
        gel = sb("gel", 2, CH)
        amp = sb("amp", 2, CH)
        diag = sb("diag", NDIAG, P)

        bank = [ctx.enter_context(nc.psum_tensor(f"bank{i}", [P, 512], f32)) for i in range(BANKS)]
        ysum = ctx.enter_context(nc.psum_tensor("ysum", [P, DM], f32))

        s_const = sem("s_const")
        s_xin = sem("s_xin")
        s_w = [sem(f"s_w{i}") for i in range(WS)]
        s_ready = sem("s_ready")
        s_done = {"act": sem("s_done_act"), "dve": sem("s_done_dve")}
        s_prep = sem("s_prep")
        s_lsum = sem("s_lsum")
        s_lexp = sem("s_lexp")
        s_lam = sem("s_lam")
        s_sd = sem("s_sd")
        s_xn = sem("s_xn")
        s_sq = sem("s_sq")
        s_nrm = sem("s_nrm")
        s_pd = sem("s_pd")
        s_cv = sem("s_cv")
        s_nb = sem("s_nb")
        s_ex = sem("s_ex")
        s_pw = sem("s_pw")
        s_g = [sem(f"s_g{i}") for i in range(SLOTS)]
        s_idx = sem("s_idx")
        s_gm = sem("s_gm")
        s_ge = sem("s_ge")
        s_h = sem("s_h")
        s_gl = sem("s_gl")
        s_a = sem("s_a")
        s_dg = sem("s_dg")
        s_yc = sem("s_yc")
        s_x = sem("s_x")
        s_chain = sem("s_chain")
        s_out = sem("s_out")

        def ready(eng, m, name):
            eng.wait_ge(s_ready, m * NJOBS + JOB_AT[name] + 1)

        def done(eng, m, name):
            by = JOB_BY[name]
            eng.wait_ge(s_done[by], m * JOBS_OF[by] + JOB_NTH[name])

        def bank_of(m, name):
            return bank[(m * NJOBS + JOB_AT[name]) % BANKS]

        ident = cc[:, CC_ID:CC_ID + P]
        ones64 = cc[:, CC_O64:CC_O64 + P]
        ones32 = cc[:, CC_O32:CC_O32 + P]
        eps = cc[:, CC_EPS:CC_EPS + 1]
        CONSTS = 16 * 6

        def zcol(layer, first):
            return small[:, layer, first:first + 1]

        def z_home(i, half):
            c = half * HALF
            if i == ZKB:
                return kB[:, c:c + HALF]
            if i in ZKD:
                return kD[:, i - ZKD[0], c:c + HALF]
            if i in ZP:
                return pT[:, i - ZP[0], PAD + c:PAD + c + HALF]
            order = ZQB + ZQD + ZH + ZG + ZC
            return zt[:, order.index(i), :]

        def interleave(gen, peer):
            total, ran = SLICES, 0
            for c, _ in enumerate(peer):
                if gen is None:
                    continue
                while ran < total and ran * CHUNKS < (c + 1) * total:
                    next(gen)
                    ran += 1
            if gen is not None:
                for _ in gen:
                    pass

        block = ctx.enter_context(nc.Block())

        @block.sync
        def _(sp):
            sp.dma_start(x[:, :, :], x_d.rearrange("(t p) d -> p t d", p=P)).then_inc(s_xin, 16)
            sp.dma_start(cc[:, :], consts_d).then_inc(s_const, 16)
            sp.dma_start(small[:, :, :], small_d).then_inc(s_const, 16)

            def load_w(n):
                m, b = divmod(n, WBLOCKS)
                if n >= WS:
                    pm, pb = divmod(n - WS, WBLOCKS)
                    ready(sp, pm, W_JOB[pb])
                sp.dma_start(w[:, n % WS, :, :], wall_d[m // 2, b]).then_inc(s_w[n % WS], 16)

            for n in range(WS):
                load_w(n)
            sp.dma_start(wpool[:, :, :, :], wpool_d).then_inc(s_const, 16)
            sp.dma_start(skt[:, :, :, :], skt_d).then_inc(s_const, 16)
            for layer in range(DEPTH):
                sp.dma_start(g2b[:, layer, :], g2b_d[layer]).then_inc(s_const, 16)
            for n in range(WS, NBLK * WBLOCKS):
                load_w(n)
            first = SEQ // P * (DEPTH - 1)
            for t in range(SEQ // P):
                sp.wait_ge(s_x, first + t + 1)
                sp.dma_start(out_d[t * P:(t + 1) * P, :], x[:, t, :]).then_inc(s_out, 16)
            sp.wait_ge(s_out, 16 * (SEQ // P))

        @block.gpsimd
        def _(pool):
            for m in range(NBLK):
                for head in range(TT * HEADS):
                    g = m * TT * HEADS + head
                    pool.wait_ge(s_idx, g + 1)
                    for k in range(TOPK):
                        n = g * TOPK + k
                        if n >= SLOTS:
                            pool.wait_ge(s_yc, n - SLOTS + 1)
                        pool.indirect_dma_start(
                            gather[:, n % SLOTS, :], None, uv_d[m // 2],
                            bass.IndirectOffsetOnAxis(ap=idx[:, g % 2, k:k + 1], axis=0)
                        ).then_inc(s_g[n % SLOTS], 16)

        def mixer_pe(pe, m):
            layer, half = divmod(m, 2)
            t0 = half * TT

            def start(name):
                n = m * NJOBS + JOB_AT[name]
                if n >= BANKS:
                    pm, pj = divmod(n - BANKS, NJOBS)
                    done(pe, pm, JOBS[pj][0])
                return bank_of(m, name)

            def weights(b):
                n = m * WBLOCKS + b
                pe.wait_ge(s_w[n % WS], 16 * (n // WS + 1))
                return w[:, n % WS, :, :]

            def transposes(kind, which):
                for t in range(TT):
                    pe.wait_ge(s_xn, 4 * m + which + t + 1)
                    for h in range(2):
                        ps = start((kind, t, h))
                        for k in range(4):
                            d = 4 * h + k
                            mm = nc.tensor.transpose(ps[:, k * P:(k + 1) * P], xn[:, t, d * P:(d + 1) * P], ident)
                        mm.then_inc(s_ready, 1)
                    yield

            def project(name, b):
                wt = weights(b)
                ps = start(name)
                for d in range(KD):
                    mm = nc.tensor.matmul(ps[:, 0:HALF], wt[:, d, :], xnT[:, d, :], start=d == 0, stop=d == KD - 1)
                mm.then_inc(s_ready, 1)

            if m == 0:
                pe.wait_ge(s_const, CONSTS)
            yield from transposes("xT", 0)
            done(pe, m, ("xT", TT - 1, 1))
            for i in range(NORMED):
                project(("z", i), i)
                yield
            for i in range(NV):
                wt = weights(NORMED + i)
                ps = start(("v", i))
                for t in range(TT):
                    for d in range(KD):
                        mm = nc.tensor.matmul(ps[:, t * P:(t + 1) * P], xnT[:, d, t * P:(t + 1) * P], wt[:, d, :],
                                              start=d == 0, stop=d == KD - 1)
                mm.then_inc(s_ready, 1)
                yield
            for i in range(NORMED, NZ):
                project(("z", i), NV + i)
                if i > NORMED:
                    n = i - NORMED - 1
                    ps = start(("n", n))
                    pe.wait_ge(s_sq, 15 * m + n + 1)
                    nc.tensor.matmul(ps[:, 0:HALF], ones64 if n <= ZKB else ones32, sq[:, (15 * m + n) % 2, :],
                                     start=True, stop=True).then_inc(s_ready, 1)
                yield

            def attn_scores(a):
                swa, t, h, k0 = item(a, t0)
                tq, keys = (t - t0) * P, slice(k0 * P, (t + 1) * P)
                for mp in range(1 if swa else 2):
                    ps = start(("s", a, mp))
                    if swa:
                        rows = slice(64 * (h // 2), 64 * (h // 2) + 64)
                        q, k = zt[rows, h % 2, tq:tq + P], kB[rows, keys]
                    else:
                        row = 64 * (h % 2) + 32 * mp
                        rows = slice(row, row + 32)
                        q, k = zt[rows, 2 + h // 2, tq:tq + P], kD[rows, h // 2, keys]
                    nc.tensor.matmul(ps[:, 0:(t + 1 - k0) * P], q, k, start=True, stop=True).then_inc(s_ready, 1)

            pe.wait_ge(s_nrm, 15 * m + NORMED)
            attn_scores(0)
            attn_scores(1)
            yield
            for a in range(ITEMS + 1):
                if a < ITEMS:
                    swa, t, h, k0 = item(a, t0)
                    ps = start(("t", a))
                    pe.wait_ge(s_pw, ITEMS * m + a + 1)
                    for b in range(t + 1 - k0):
                        mm = nc.tensor.transpose(ps[:, b * P:(b + 1) * P], sc[:, a % 2, 0, b * P:(b + 1) * P], ident)
                    mm.then_inc(s_ready, 1)
                    if a + 2 < ITEMS:
                        attn_scores(a + 2)
                if a:
                    swa, t, h, k0 = item(a - 1, t0)
                    ps = start(("o", a - 1))
                    done(pe, m, ("t", a - 1))
                    col = (h // 2) * 64 if swa else P + h * 64
                    rows = slice(64 * (h % 2), 64 * (h % 2) + 64)
                    n = t + 1 - k0
                    for b in range(n):
                        mm = nc.tensor.matmul(ps[rows, 0:P], vAll[:, k0 + b, col:col + 64],
                                              pt[:, (a - 1) % 2, b * P:(b + 1) * P], start=b == 0, stop=b == n - 1)
                    mm.then_inc(s_ready, 1)
                yield
            for j in range(2):
                ps = start(("pool", j))
                pe.wait_ge(s_pd, 2 * m + j + 1)
                nc.tensor.matmul(ps[:, 0:HALF], wpool[:, layer, j, :], pd[:, j, :], start=True, stop=True)\
                    .then_inc(s_ready, 1)
            yield
            for n in range(8):
                ps = start(("y", n))
                pe.wait_ge(s_sq, 15 * m + NORMED + n + 1)
                nc.tensor.matmul(ps[:, 0:HALF], ones64, sq[:, (15 * m + NORMED + n) % 2, :], start=True, stop=True)\
                    .then_inc(s_ready, 1)
                yield
            pe.wait_ge(s_nrm, 15 * m + 15)
            for i in range(8):
                wt = weights(NZ + NV + i)
                ps = start(("out", i))
                for t in range(TT):
                    for c in range(8):
                        mm = nc.tensor.matmul(ps[:, t * P:(t + 1) * P], yT[:, c, t * P:(t + 1) * P], wt[:, c, :],
                                              start=c == 0, stop=c == 7)
                mm.then_inc(s_ready, 1)
                yield
            yield from transposes("x2T", 2)
            done(pe, m, ("x2T", TT - 1, 1))
            for i in range(16):
                project(("q", i), NZ + NV + 8 + i)
                yield
            for t in range(TT):
                for g in range(4):
                    ps = start(("sk", t, g))
                    done(pe, m, ("q", 4 * g + 3))
                    for k in range(4):
                        hc = 4 * g + k
                        mm = nc.tensor.matmul(ps[:, k * P:(k + 1) * P], qT[:, hc, t * P:(t + 1) * P],
                                              skt[:, layer, hc % 2, :], start=True, stop=True)
                    mm.then_inc(s_ready, 1)
                    yield

        def chunk_pe(pe, c):
            for j in range(CH):
                n = c * CH + j
                k = n % (HEADS * TOPK)
                if k == 0 and n:
                    pe.wait_ge(s_x, n // (HEADS * TOPK))
                pe.wait_ge(s_dg, n + 1)
                for hf in range(2):
                    mm = nc.tensor.matmul(ysum[:, hf * 512:(hf + 1) * 512], diag[:, n % NDIAG, :],
                                          gather[:, n % SLOTS, DM + hf * 512:DM + (hf + 1) * 512],
                                          start=k == 0, stop=k == HEADS * TOPK - 1)
                mm.then_inc(s_yc, 1)

        def peer_pe(pe, m):
            for c in range(CHUNKS):
                if c:
                    chunk_pe(pe, m * CHUNKS + c - 1)
                yield
            chunk_pe(pe, (m + 1) * CHUNKS - 1)

        @block.tensor
        def _(pe):
            for _ in mixer_pe(pe, 0):
                pass
            for m in range(NBLK):
                interleave(mixer_pe(pe, m + 1) if m + 1 < NBLK else None, peer_pe(pe, m))

        def mixer_act(act, m):
            layer, half = divmod(m, 2)
            t0 = half * TT
            mean = 1.0 / DM

            def x_rms(which):
                for t in range(TT):
                    nc.scalar.activation(xn[:, t, :], x[:, t0 + t, :], ACT.Square, accum_out=ss[:, which + t:which + t + 1])\
                        .then_inc(s_actc, 1)
                    actc[0] += 1
                    act.wait_ge(s_actc, actc[0])
                    nc.scalar.activation(sdv[:, which + t:which + t + 1], ss[:, which + t:which + t + 1], ACT.Sqrt,
                                         bias=eps, scale=mean).then_inc(s_sd, 1)
                    yield

            def square(n, src):
                nn = 15 * m + n
                if nn >= 2:
                    pm, pn = divmod(nn - 2, 15)
                    ready(act, pm, ("n", pn) if pn < NORMED else ("y", pn - NORMED))
                nc.scalar.activation(sq[:, nn % 2, :], src, ACT.Square).then_inc(s_sq, 1)

            def root(name, n, width):
                nn = 15 * m + n
                ready(act, m, name)
                if nn >= 2:
                    act.wait_ge(s_nrm, nn - 1)
                nc.scalar.activation(sd[:, nn % 2, :], bank_of(m, name)[:, 0:HALF], ACT.Sqrt, bias=eps,
                                     scale=1.0 / width).then_inc(s_done["act"], 1)

            def empty(name, out, in_):
                ready(act, m, name)
                nc.scalar.activation(out, in_, ACT.Copy).then_inc(s_done["act"], 1)

            if m == 0:
                act.wait_ge(s_xin, 16)
                act.wait_ge(s_const, CONSTS)
            elif layer:
                act.wait_ge(s_x, 2 * m - 2)
            if m:
                ready(act, m - 1, ("x2T", TT - 1, 1))
            yield from x_rms(0)
            for i in range(NORMED):
                empty(("z", i), z_home(i, half), bank_of(m, ("z", i))[:, 0:HALF])
                yield
            for i in range(NV):
                empty(("v", i), vAll[:, t0:t0 + TT, i * P:(i + 1) * P],
                      bank_of(m, ("v", i))[:, 0:HALF].rearrange("p (t c) -> p t c", t=TT))
                yield
            done(act, m, ("z", NORMED - 1))
            if m == 0:
                act.wait_ge(s_prep, 2)
            for i in range(NORMED, NZ):
                empty(("z", i), z_home(i, half), bank_of(m, ("z", i))[:, 0:HALF])
                n = i - NORMED
                if n < NORMED:
                    square(n, z_home(n, half))
                if n:
                    root(("n", n - 1), n - 1, 64 if n - 1 <= ZKB else 32)
                yield

            def attn_exp(a):
                swa, t, h, k0 = item(a, t0)
                s, cols = a % 2, (t + 1 - k0) * P
                act.wait_ge(s_nb, ITEMS * m + a + 1)
                scale = (64 ** -0.5) * slope(h) if swa else (32 ** -0.5) * slope(4 + h)
                for mp in range(1 if swa else 2):
                    e = nc.scalar.activation(sc[:, s, mp, 0:cols], sc[:, s, mp, 0:cols], ACT.Exp,
                                             bias=st[:, s, 2 + mp:3 + mp], scale=scale,
                                             accum_out=st[:, s, 4 + mp:5 + mp])
                if swa:
                    e = nc.scalar.activation(st[:, s, 6:7], small[:, layer, SP_SINK + h:SP_SINK + h + 1], ACT.Exp,
                                             bias=st[:, s, 2:3])
                e.then_inc(s_ex, 1)

            attn_exp(0)
            yield
            for a in range(ITEMS + 1):
                if a < ITEMS:
                    swa, t, h, k0 = item(a, t0)
                    cols = (t + 1 - k0) * P
                    if a + 1 < ITEMS:
                        attn_exp(a + 1)
                    ready(act, m, ("t", a))
                    nc.scalar.activation(pt[:, a % 2, 0:cols], bank_of(m, ("t", a))[:, 0:cols], ACT.Copy)\
                        .then_inc(s_done["act"], 1)
                if a:
                    swa, t, h, k0 = item(a - 1, t0)
                    rows = slice(64 * (h % 2), 64 * (h % 2) + 64)
                    empty(("o", a - 1), yT[rows, (2 if swa else 6) + h // 2, (t - t0) * P:(t - t0 + 1) * P],
                          bank_of(m, ("o", a - 1))[rows, 0:P])
                yield
            for j in range(2):
                empty(("pool", j), yT[:, j, :], bank_of(m, ("pool", j))[:, 0:HALF])
            yield
            act.wait_ge(s_cv, 2 * m + 2)
            done(act, m, ("pool", 1))
            for n in range(8):
                if n == 0:
                    square(NORMED, yT[:, YORDER[0], :])
                if n + 1 < 8:
                    square(NORMED + n + 1, yT[:, YORDER[n + 1], :])
                root(("y", n), NORMED + n, 64)
                yield
            for i in range(8):
                yield
            done(act, m, ("out", 7))
            yield from x_rms(2)
            for i in range(16):
                empty(("q", i), qT[:, i, :], bank_of(m, ("q", i))[:, 0:HALF])
                yield
            if m:
                act.wait_ge(s_idx, TT * HEADS * m)
            for t in range(TT):
                for g in range(4):
                    empty(("sk", t, g), scores[:, t, 4 * g:4 * g + 4, :],
                          bank_of(m, ("sk", t, g))[:, :].rearrange("p (c k) -> p c k", c=4))
                    yield

        def gate_exp(act, g):
            act.wait_ge(s_gm, g + 1)
            nc.scalar.activation(gate_e[:, :], best_v[:, :], ACT.Exp, bias=neg_best[:, :],
                                 accum_out=gate_s[:, 0:1]).then_inc(s_ge, 1)

        def diagonals(act, c):
            act.wait_ge(s_a, c + 1)
            for j in range(CH):
                n = c * CH + j
                if n >= NDIAG:
                    act.wait_ge(s_yc, n - NDIAG + 1)
                nc.scalar.activation(diag[:, n % NDIAG, :], ident, ACT.Copy, scale=amp[:, c % 2, j:j + 1]).then_inc(s_dg, 1)

        def peer_act(act, m):
            for c in range(CHUNKS):
                cg = m * CHUNKS + c
                act.wait_ge(s_h, cg + 1)
                nc.scalar.activation(gel[:, cg % 2, :], hdot[:, cg % 2, :], ACT.Gelu).then_inc(s_gl, 1)
                if c:
                    diagonals(act, cg - 1)
                if c % 4 == 1 and c // 4 + 1 < TT * HEADS:
                    gate_exp(act, m * TT * HEADS + c // 4 + 1)
                yield
            diagonals(act, (m + 1) * CHUNKS - 1)

        actc = [0]
        s_actc = sem("s_actc")

        @block.scalar
        def _(act):
            act.wait_ge(s_lsum, 1)
            nc.scalar.activation(lam_e[:, :, :], lam_s[:, :, :], ACT.Exp).then_inc(s_lexp, 1)
            for _ in mixer_act(act, 0):
                pass
            for m in range(NBLK):
                gate_exp(act, m * TT * HEADS)
                interleave(mixer_act(act, m + 1) if m + 1 < NBLK else None, peer_act(act, m))

        V = nc.vector
        chained = [0]

        def chain(dve, ins):
            chained[0] += 1
            ins.then_inc(s_chain, 1)
            dve.wait_ge(s_chain, chained[0])

        def mixer_dve(dve, m):
            layer, half = divmod(m, 2)
            t0 = half * TT

            def normalise_x(which, kind, gain, rr):
                for t in range(TT):
                    dve.wait_ge(s_sd, 4 * m + which + t + 1)
                    chain(dve, V.reciprocal(rr[t], sdv[:, which + t:which + t + 1]))
                    V.tensor_scalar(xn[:, t, :], x[:, t0 + t, :], rr[t], None, ALU.mult).then_inc(s_xn, 1)
                    for h in range(2):
                        ready(dve, m, (kind, t, h))
                        V.tensor_tensor(
                            xnT[:, 4 * h:4 * h + 4, t * P:(t + 1) * P],
                            bank_of(m, (kind, t, h))[:, :].rearrange("p (k c) -> p k c", k=4),
                            small[:, layer, gain + 4 * h:gain + 4 * h + 4].unsqueeze(2).to_broadcast([P, 4, P]),
                            ALU.mult).then_inc(s_done["dve"], 1)
                    yield

            def normalise(n, tile, gain):
                nn = 15 * m + n
                done(dve, m, ("n", n) if n < NORMED else ("y", n - NORMED))
                chain(dve, V.reciprocal(sd[:, nn % 2, :], sd[:, nn % 2, :]))
                V.scalar_tensor_tensor(tile, tile, gain, sd[:, nn % 2, :], ALU.mult, ALU.mult).then_inc(s_nrm, 1)

            if m == 0:
                dve.wait_ge(s_xin, 16)
            elif layer:
                dve.wait_ge(s_x, 2 * m - 2)
            yield from normalise_x(0, "xT", SP_G1, [r1[:, t:t + 1] for t in range(TT)])
            for i in range(NORMED + NV):
                yield
            for i in range(NORMED, NZ):
                n = i - NORMED
                if n:
                    normalise(n - 1, z_home(n - 1, half), zcol(layer, SP_QKG + n - 1))
                yield

            def attn_bias(a):
                swa, t, h, k0 = item(a, t0)
                s, cols = a % 2, (t + 1 - k0) * P
                scale = (64 ** -0.5) * slope(h) if swa else (32 ** -0.5) * slope(4 + h)
                for mp in range(1 if swa else 2):
                    ready(dve, m, ("s", a, mp))
                    bias = cc[:, CC_DB + 256 - cols:CC_DB + 256] if swa else cc[:, CC_DD + 512 - cols:CC_DD + 512]
                    V.tensor_tensor_reduce(out=sc[:, s, mp, 0:cols], in0=bank_of(m, ("s", a, mp))[:, 0:cols], in1=bias,
                                           scale=1.0, scalar=-BIG, op0=ALU.add, op1=ALU.max,
                                           accum_out=st[:, s, mp:mp + 1]).then_inc(s_done["dve"], 1)
                done(dve, m, ("s", a, 0 if swa else 1))
                if swa:
                    chain(dve, V.tensor_scalar(st[:, s, 0:1], st[:, s, 0:1], scale, None, ALU.mult))
                    chain(dve, V.tensor_tensor(st[:, s, 0:1], st[:, s, 0:1],
                                               small[:, layer, SP_SINK + h:SP_SINK + h + 1], ALU.max))
                    V.tensor_scalar(st[:, s, 2:3], st[:, s, 0:1], -1.0, None, ALU.mult).then_inc(s_nb, 1)
                else:
                    V.tensor_scalar(st[:, s, 2:4], st[:, s, 0:2], -scale, None, ALU.mult).then_inc(s_nb, 1)

            def attn_weights(a):
                swa, t, h, k0 = item(a, t0)
                s, cols = a % 2, (t + 1 - k0) * P
                dve.wait_ge(s_ex, ITEMS * m + a + 1)
                if swa:
                    chain(dve, V.tensor_tensor(st[:, s, 7:8], st[:, s, 4:5], st[:, s, 6:7], ALU.add))
                    chain(dve, V.reciprocal(st[:, s, 8:9], st[:, s, 7:8]))
                    V.tensor_scalar(sc[:, s, 0, 0:cols], sc[:, s, 0, 0:cols], st[:, s, 8:9], None, ALU.mult)\
                        .then_inc(s_pw, 1)
                else:
                    chain(dve, V.reciprocal(st[:, s, 8:10], st[:, s, 4:6]))
                    chain(dve, V.tensor_tensor(st[:, s, 10:11], st[:, s, 9:10], neg_lam[:, layer:layer + 1], ALU.mult))
                    chain(dve, V.tensor_scalar(sc[:, s, 0, 0:cols], sc[:, s, 0, 0:cols], st[:, s, 8:9], None, ALU.mult))
                    V.scalar_tensor_tensor(sc[:, s, 0, 0:cols], sc[:, s, 1, 0:cols], st[:, s, 10:11],
                                           sc[:, s, 0, 0:cols], ALU.mult, ALU.add).then_inc(s_pw, 1)

            c0 = half * HALF
            done(dve, m, ("z", ZP[1]))
            for j in range(2):
                src = pT[:, j, c0:c0 + PAD + HALF]
                for lv in range(2 if j == 0 else 4):
                    sh = 1 << lv
                    lo = 2 * sh - 1
                    chain(dve, V.tensor_tensor(pool_sum[:, lv, lo:PAD + HALF], src[:, lo:PAD + HALF],
                                               src[:, lo - sh:PAD + HALF - sh], ALU.add))
                    src = pool_sum[:, lv, :]
                for part in range(2):
                    rows = slice(64 * part, 64 * part + 64)
                    lv = 2 * j + part
                    if half == 0:
                        chain(dve, V.tensor_tensor(pool_sum[rows, lv, PAD:2 * PAD], pool_sum[rows, lv, PAD:2 * PAD],
                                                   cc[rows, CC_CORR + PAD * j:CC_CORR + PAD * (j + 1)], ALU.mult))
                    e = V.scalar_tensor_tensor(pd[rows, j, :], pool_sum[rows, lv, PAD:PAD + HALF],
                                               cc[rows, CC_INVW + j:CC_INVW + j + 1],
                                               pT[rows, j, PAD + c0:PAD + c0 + HALF], ALU.mult, ALU.subtract)
                    if part:
                        e.then_inc(s_pd, 1)
                    else:
                        chain(dve, e)
            dve.wait_ge(s_pd, 2 * m + 2)
            attn_bias(0)
            attn_bias(1)
            yield
            for a in range(ITEMS + 1):
                if a < ITEMS:
                    attn_weights(a)
                    if a + 2 < ITEMS:
                        ready(dve, m, ("t", a))
                        attn_bias(a + 2)
                yield
            done(dve, m, ("z", NZ - 1))
            for j in range(2):
                hh, gg, cg = (z_home(z[j], half) for z in (ZH, ZG, ZC))
                yc = yT[:, 4 + j, :]
                chain(dve, V.tensor_tensor(cT[:, j, PAD + c0:PAD + c0 + HALF], cg, hh, ALU.mult))
                tap = [cT[:, j, PAD + c0 - 2 + k:PAD + c0 - 2 + k + HALF] for k in range(3)]
                wc = [zcol(layer, SP_CONV + 2 * k + j) for k in range(3)]
                chain(dve, V.tensor_scalar(yc, tap[0], wc[0], None, ALU.mult))
                chain(dve, V.scalar_tensor_tensor(yc, tap[1], wc[1], yc, ALU.mult, ALU.add))
                chain(dve, V.scalar_tensor_tensor(yc, tap[2], wc[2], yc, ALU.mult, ALU.add))
                V.tensor_tensor(yc, yc, gg, ALU.mult).then_inc(s_cv, 1)
            yield
            for n in range(8):
                y = YORDER[n]
                normalise(NORMED + n, yT[:, y, :], zcol(layer, SP_OG + y))
                yield
            for i in range(8):
                ready(dve, m, ("out", i))
                V.tensor_tensor(x[:, t0:t0 + TT, i * P:(i + 1) * P],
                                bank_of(m, ("out", i))[:, 0:HALF].rearrange("p (t c) -> p t c", t=TT),
                                x[:, t0:t0 + TT, i * P:(i + 1) * P], ALU.add).then_inc(s_done["dve"], 1)
                yield
            done(dve, m, ("out", 7))
            yield from normalise_x(2, "x2T", SP_G2, [r2[:, t0 + t:t0 + t + 1] for t in range(TT)])
            for i in range(16 + 4 * TT):
                yield

        def top16(dve, vals, spare, tv, ti):
            chain(dve, V.max(tv[:, 0:8], vals))
            V.max_index(ti[:, 0:8], tv[:, 0:8], vals)
            chain(dve, V.match_replace(spare, tv[:, 0:8], vals, -BIG))
            chain(dve, V.max(tv[:, 8:16], spare))
            chain(dve, V.max_index(ti[:, 8:16], tv[:, 8:16], spare))

        def route_keys(dve, m, head):
            t, h = divmod(head, HEADS)
            if head % HEADS == 0 and head // HEADS < TT:
                done(dve, m, ("sk", t, 3))
            for c in range(2):
                top16(dve, scores[:, t, 2 * h + c, :], sc2[:, c, :], top_v[:, c, :], top_i[:, c, :])
            V.tensor_copy(top_f[:, :, :], top_i[:, :, :])
            chain(dve, V.tensor_tensor(cand[:, :, :], top_v[:, 0, :].unsqueeze(2).to_broadcast([P, TOPK, TOPK]),
                                       top_v[:, 1, :].unsqueeze(1).to_broadcast([P, TOPK, TOPK]), ALU.add))

        def route_experts(dve, m, head):
            g = m * TT * HEADS + head
            flat = lambda c: c[:, :, :].rearrange("p a b -> p (a b)")
            if g:
                dve.wait_ge(s_ge, g)
            top16(dve, flat(cand), flat(cand2), best_v, best_p)
            V.tensor_scalar(neg_best[:, :], best_v[:, 0:1], -1.0, None, ALU.mult).then_inc(s_gm, 1)
            V.tensor_scalar(pos_u[:, 0, :], best_p[:, :], 4, None, ALU.logical_shift_right)
            chain(dve, V.tensor_scalar(pos_u[:, 1, :], best_p[:, :], 15, None, ALU.bitwise_and))
            chain(dve, V.tensor_copy(pos_f[:, :, :], pos_u[:, :, :]))
            both = [P, 2 * TOPK, TOPK]
            chain(dve, V.tensor_tensor(
                hot[:, :, :], pos_f[:, :, :].rearrange("p c k -> p (c k)").unsqueeze(2).to_broadcast(both),
                cc[:, CC_IOTA:CC_IOTA + TOPK].unsqueeze(1).to_broadcast(both), ALU.is_equal))
            hot4 = hot[:, :, :].rearrange("p (c k) a -> p c k a", c=2)
            chain(dve, V.tensor_tensor(hot4, hot4, top_f[:, :, :].unsqueeze(2).to_broadcast([P, 2, TOPK, TOPK]), ALU.mult))
            chain(dve, V.tensor_reduce(ij[:, :, :].rearrange("p c k -> p (c k)"), hot[:, :, :], AX, ALU.add))
            V.scalar_tensor_tensor(idx[:, g % 2, :], ij[:, 0, :], float(NKEYS), ij[:, 1, :], ALU.mult, ALU.add)\
                .then_inc(s_idx, 1)

        def route_gate(dve, m, head):
            g = m * TT * HEADS + head
            dve.wait_ge(s_ge, g + 1)
            chain(dve, V.reciprocal(gate_s[:, 1:2], gate_s[:, 0:1]))
            chain(dve, V.tensor_scalar(gate[:, g % 2, :], gate_e[:, :], gate_s[:, 1:2], None, ALU.mult))

        def peer_dve(dve, m):
            layer = m // 2
            last = (m + 1) * CHUNKS - 1

            def weigh(cg):
                dve.wait_ge(s_gl, cg + 1)
                if cg >= 2:
                    dve.wait_ge(s_dg, CH * (cg - 1))
                k = cg % 4 * CH
                V.tensor_tensor(amp[:, cg % 2, :], gel[:, cg % 2, :], gate[:, cg // 4 % 2, k:k + CH], ALU.mult)\
                    .then_inc(s_a, 1)

            def add_tile(tg):
                dve.wait_ge(s_yc, (tg + 1) * HEADS * TOPK)
                t = tg % (SEQ // P)
                V.tensor_tensor(x[:, t, :], ysum[:, :], x[:, t, :], ALU.add).then_inc(s_x, 1)

            per_tile = CHUNKS // TT
            for c in range(CHUNKS):
                cg = m * CHUNKS + c
                t = (m % 2) * TT + c // per_tile
                head = c // 4
                if c % per_tile == 0:
                    if c == 0:
                        done(dve, m, ("out", 7))
                    chain(dve, V.scalar_tensor_tensor(xc[:, :], x[:, t, :], r2[:, t:t + 1], g2b[:, layer, :],
                                                      ALU.mult, ALU.mult))
                for j in range(CH):
                    n = cg * CH + j
                    dve.wait_ge(s_g[n % SLOTS], 16 * (n // SLOTS + 1))
                    e = V.tensor_tensor_reduce(out=gather[:, n % SLOTS, 0:DM], in0=gather[:, n % SLOTS, 0:DM],
                                               in1=xc[:, :], scale=1.0, scalar=0.0, op0=ALU.mult, op1=ALU.add,
                                               accum_out=hdot[:, cg % 2, j:j + 1])
                    if j == CH - 1:
                        e.then_inc(s_h, 1)
                if c:
                    weigh(cg - 1)
                if c == per_tile + 1:
                    add_tile(m * TT)
                if head + 1 < TT * HEADS:
                    if c % 4 == 0:
                        route_keys(dve, m, head + 1)
                    elif c % 4 == 1:
                        route_experts(dve, m, head + 1)
                    elif c % 4 == 3:
                        route_gate(dve, m, head + 1)
                yield
            weigh(last)
            add_tile(m * TT + 1)

        @block.vector
        def _(dve):
            V.memset(pT[:, :, 0:PAD], 0.0).then_inc(s_prep, 1)
            V.memset(cT[:, :, 0:PAD], 0.0).then_inc(s_prep, 1)
            dve.wait_ge(s_const, CONSTS)
            for layer in range(DEPTH):
                lam = small[:, layer, SP_LAM:SP_LAM + 128].rearrange("p (a b k) -> p a b k", a=2, b=2)
                chain(dve, V.tensor_tensor(lam_t[:, layer, :, :], lam[:, :, 0, :], lam[:, :, 1, :], ALU.mult))
                for n, i in enumerate(ZQB + ZQD):
                    gcol = zcol(layer, SP_QKG + i)
                    chain(dve, V.tensor_tensor(gcol, gcol, cc[:, CC_SLI + n:CC_SLI + n + 1], ALU.mult))
                og = small[:, layer, SP_OG + 6:SP_OG + 8]
                chain(dve, V.tensor_scalar(og, og, 1.0 - lam_init(layer), None, ALU.mult))
            V.tensor_reduce(lam_s[:, :, :], lam_t[:, :, :, :], AX, ALU.add).then_inc(s_lsum, 1)
            dve.wait_ge(s_lexp, 1)
            for layer in range(DEPTH):
                chain(dve, V.tensor_tensor(neg_lam[:, layer:layer + 1], lam_e[:, layer, 1:2], lam_e[:, layer, 0:1],
                                           ALU.subtract))
                chain(dve, V.tensor_scalar(neg_lam[:, layer:layer + 1], neg_lam[:, layer:layer + 1],
                                           -lam_init(layer), None, ALU.add))
            for _ in mixer_dve(dve, 0):
                pass
            for m in range(NBLK):
                route_keys(dve, m, 0)
                route_experts(dve, m, 0)
                route_gate(dve, m, 0)
                interleave(mixer_dve(dve, m + 1) if m + 1 < NBLK else None, peer_dve(dve, m))


SLICES = 2 + NZ + NV + 1 + ITEMS + 1 + 1 + 8 + 8 + 2 + 16 + 8


def columns():
    a, qb, kb, vb, h, b, c, qd, kd, vd = np.cumsum([0, 256, 256, 128, 128, 256, 256, 256, 256, 256])
    r = np.arange
    heads = lambda first, hs: np.concatenate([first + 64 * h + r(64) for h in hs])
    tiles = [heads(qb, (0, 2)), heads(qb, (1, 3)), kb + r(128), qd + r(128), qd + 128 + r(128),
             kd + r(128), kd + 128 + r(128), vb + r(128), vd + r(128), vd + 128 + r(128),
             a + r(128), a + 128 + r(128)]
    for first in (h, b, c):
        tiles += [first + r(128), first + 128 + r(128)]
    return np.concatenate(tiles)


def layout_weights(w_in, w_out, w_query):
    both = np.concatenate([w_in[:, :, columns()], w_out, w_query], axis=2)
    tiled = both.reshape(DEPTH, KD, P, WBLOCKS, P)
    return np.ascontiguousarray(tiled.transpose(0, 3, 2, 1, 4))


def layout_small(i):
    out = np.zeros((P, DEPTH, SP_N), np.float32)
    for l in range(DEPTH):
        s = out[:, l]
        s[:, SP_G1:SP_G1 + 8] = i["norm1_g"][l].reshape(8, P).T
        s[:, SP_G2:SP_G2 + 8] = i["norm2_g"][l].reshape(8, P).T
        s[:, SP_OG:SP_OG + 8] = i["out_norm_g"][l].reshape(8, P).T
        for n, name in enumerate(["swa_q_norm"] * 2 + ["swa_k_norm"] + ["diff_q_norm"] * 2 + ["diff_k_norm"] * 2):
            g = i[name][l]
            s[:, SP_QKG + n] = np.tile(g, P // g.size)
        for k in range(3):
            for j in range(2):
                s[:, SP_CONV + 2 * k + j] = i["conv_w"][l, k, j * P:(j + 1) * P]
        s[:, SP_SINK:SP_SINK + 4] = i["swa_sinks"][l][None]
        s[:, SP_LAM:SP_LAM + 128] = np.concatenate([i[n][l] for n in ("lam_q1", "lam_k1", "lam_q2", "lam_k2")])[None]
    return out


def layout_consts():
    c = np.zeros((P, CC_N), np.float32)
    q = np.arange(P)[:, None]
    c[:, CC_ID:CC_ID + P] = np.eye(P)
    c[:, CC_O64:CC_O64 + P] = q // 64 == np.arange(P)[None] // 64
    c[:, CC_O32:CC_O32 + P] = q // 32 == np.arange(P)[None] // 32
    dist = q + 128 - np.arange(256)[None]
    c[:, CC_DB:CC_DB + 256] = np.where((dist >= 0) & (dist < 128), -dist * math.sqrt(64), MASK)
    dist = q + 384 - np.arange(512)[None]
    c[:, CC_DD:CC_DD + 512] = np.where(dist >= 0, -dist * math.sqrt(32), MASK)
    c[:, CC_IOTA:CC_IOTA + TOPK] = np.arange(TOPK)[None]
    for j in range(2):
        for part in range(2):
            win = 2 ** (2 * j + part + 1)
            rows = slice(64 * part, 64 * part + 64)
            c[rows, CC_INVW + j] = 1.0 / win
            c[rows, CC_CORR + PAD * j:CC_CORR + PAD * (j + 1)] = win / np.minimum(np.arange(PAD) + 1, win)
    for rows, base in ((slice(0, 64), 0), (slice(64, 128), 1)):
        for g in range(2):
            c[rows, CC_SLI + g] = 1.0 / slope(2 * base + g)
            c[rows, CC_SLI + 2 + g] = 1.0 / slope(4 + 2 * g + base)
    c[:, CC_EPS] = EPS
    return c


def kernel(**inputs):
    import concourse.bacc as bacc
    from concourse.bass_utils import run_bass_kernel_spmd as run
    i = {k: np.asarray(v) for k, v in inputs.items()}
    wp = np.zeros((P, DEPTH, 2, P), np.float32)
    for l in range(DEPTH):
        for g in range(4):
            r = slice(64 * (g % 2), 64 * (g % 2) + 64)
            wp[r, l, g // 2, r] = i["w_pool"][l, g]
    arrays = {
        "x_in": np.ascontiguousarray(i["x"].reshape(SEQ, DM)),
        "weights": layout_weights(i["w_in"], i["w_out"], i["w_query"]),
        "small_in": layout_small(i),
        "consts_in": layout_consts(),
        "g2_rows": np.ascontiguousarray(np.broadcast_to(i["norm2_g"][:, None, :], (DEPTH, P, DM))),
        "wpool_in": wp,
        "keys_t": np.ascontiguousarray(i["sub_keys"].transpose(3, 0, 1, 2)),
    }
    for l in range(DEPTH):
        arrays[f"experts{l}"] = np.concatenate([i["peer_u"][l], i["peer_v"][l]], axis=1)
    nc = bacc.Bacc("TRN2", target_bir_lowering=False, num_devices=1)
    aps = [nc.dram_tensor(n, a.shape, mybir.dt.from_np(a.dtype), kind="ExternalInput").ap() for n, a in arrays.items()]
    out = nc.dram_tensor("y_out", (SEQ, DM), mybir.dt.float32, kind="ExternalOutput").ap()
    build(nc, *aps[:7], aps[7:], out)
    r = run(nc, [arrays], core_ids=[0])
    return r.results[0]["y_out"].reshape(1, SEQ, DM)
```

```python
import math
from contextlib import ExitStack
from itertools import chain as chain_of

import numpy as np
import concourse.bass as bass
from concourse import mybir

DEPTH, SEQ, DM = 2, 512, 1024
P = 128
HALF = 256
TT = HALF // P
NBLK = 2 * DEPTH
KD = DM // P
EPS = 1e-6
PAD = 16
HEADS, TOPK, NKEYS = 8, 16, 128
NEXP = NKEYS * NKEYS
CH = 4
CHUNKS = HEADS * TT * TOPK // CH
SLOTS = 8
NDIAG = 4
WS = 4
BIG = 3.0e38
MASK = -1.0e30

ZQB, ZKB, ZQD, ZKD = (0, 1), 2, (3, 4), (5, 6)
NORMED = 7
ZP, ZH, ZG, ZC = (7, 8), (9, 10), (11, 12), (13, 14)
NZ = 15
NV = 3
NLATE = 6
WBLOCKS = NZ + NV + 8 + 16
ITEMS = 16
YORDER = (4, 5, 2, 3, 0, 1, 6, 7)

SP_G1, SP_G2, SP_OG, SP_QKG, SP_CONV, SP_SINK, SP_LAM = 0, 8, 16, 24, 31, 37, 41
SP_N = SP_LAM + 128
CC_ID, CC_O64, CC_O32, CC_DB, CC_DD, CC_IOTA, CC_INVW, CC_CORR, CC_SLI, CC_EPS = (
    0, 128, 256, 384, 640, 1152, 1168, 1170, 1202, 1206)
CC_N = CC_EPS + 1


def slope(h):
    return 2.0 ** -(h + 1)


def lam_init(layer):
    return 0.8 - 0.6 * float(np.exp(-0.3 * layer))


def layout_jobs():
    jobs = [(("xT", t, h), "dve", None) for t in range(TT) for h in range(2)]
    for i in range(NORMED + NV):
        jobs.append((("z", i), "act", i) if i < NORMED else (("v", i - NORMED), "act", i))
        if 0 < i <= NORMED:
            jobs.append((("n", i - 1), "act", None))
    jobs += [(("z", i), "act", NV + i) for i in ZP]
    scores = lambda a: [(("s", a, k), "dve", None) for k in range(1 if a < 8 else 2)]
    jobs += scores(0) + scores(1)
    for a in range(ITEMS + 1):
        if a < ITEMS:
            jobs.append((("t", a), "act", None))
            if a + 2 < ITEMS:
                jobs += scores(a + 2)
        if a:
            jobs.append((("o", a - 1), "act", None))
        if a < NLATE:
            jobs.append((("z", ZH[0] + a), "act", NV + ZH[0] + a))
    jobs += [(("pool", j), "act", None) for j in range(2)]
    jobs += [(("y", i), "act", None) for i in range(8)]
    jobs += [(("out", i), "dve", NZ + NV + i) for i in range(8)]
    jobs += [(("x2T", t, h), "dve", None) for t in range(TT) for h in range(2)]
    for i in range(16):
        jobs.append((("q", i), "act", NZ + NV + 8 + i))
        if i % 4 == 3:
            jobs.append((("sk", 0, i // 4), "act", None))
    jobs += [(("sk", 1, g), "act", None) for g in range(4)]
    return jobs


JOBS = layout_jobs()
NJOBS = len(JOBS)
JOB_AT = {name: n for n, (name, _, _) in enumerate(JOBS)}
JOB_BY = {name: by for name, by, _ in JOBS}
JOBS_OF = {by: sum(b == by for _, b, _ in JOBS) for by in ("act", "dve")}
JOB_NTH = {name: sum(b == by for _, b, _ in JOBS[:n + 1]) for n, (name, by, _) in enumerate(JOBS)}
W_JOB = {w: name for name, _, w in JOBS if w is not None}
BANKS = 6


def item(a, t0):
    swa = a < 8
    t, h = t0 + a % 8 // 4, a % 4
    return swa, t, h, (max(t - 1, 0) if swa else 0)


def build(nc, x_d, wall_d, small_d, consts_d, g2b_d, wpool_d, skt_d, uv_d, out_d):
    f32, u32 = mybir.dt.float32, mybir.dt.uint32
    ALU, ACT, AX = mybir.AluOpType, mybir.ActivationFunctionType, mybir.AxisListType.X
    ctx = ExitStack()
    with ctx:
        def sb(name, *shape, dt=f32):
            return ctx.enter_context(nc.sbuf_tensor(name, [P, *shape], dt))

        def sem(name):
            return ctx.enter_context(nc.semaphore(name))

        x = sb("x", SEQ // P, DM)
        gather = sb("gather", SLOTS, 2 * DM)
        xnT = sb("xnT", KD, HALF)
        shared = sb("shared", 16 * HALF + 512)
        zt = shared[:, 0:10 * HALF].rearrange("p (i t) -> p i t", t=HALF)
        sc = shared[:, 10 * HALF:10 * HALF + 2048].rearrange("p (s m k) -> p s m k", s=2, m=2)
        pool_sum = shared[:, 10 * HALF:10 * HALF + 4 * (PAD + HALF)].rearrange("p (i t) -> p i t", i=4)
        qT = shared[:, 0:16 * HALF].rearrange("p (i t) -> p i t", t=HALF)
        kB = sb("kB", SEQ)
        kD = sb("kD", 2, SEQ)
        vAll = sb("vAll", SEQ // P, NV * P)
        pT = sb("pT", 2, PAD + SEQ)
        cT = sb("cT", 2, PAD + SEQ)
        pd = sb("pd", 2, HALF)
        yT = sb("yT", 8, HALF)
        xn = yT[:, :, :].rearrange("p i t -> p (i t)").rearrange("p (t d) -> p t d", t=TT)
        scores = sb("scores", TT, 16, NKEYS)
        w = sb("w", WS, KD, P)
        small = sb("small", DEPTH, SP_N)
        cc = sb("cc", CC_N)
        g2b = sb("g2b", DEPTH, DM)
        wpool = sb("wpool", DEPTH, 2, P)
        skt = sb("skt", DEPTH, 2, NKEYS)
        sq = sb("sq", 2, HALF)
        sd = sb("sd", 2, HALF)
        pt = sb("pt", 2, 512)
        ss = sb("ss", 4)
        sdv = sb("sdv", 4)
        r1 = sb("r1", TT)
        r2 = sb("r2", SEQ // P)
        st = sb("st", 2, 12)
        lam_t = sb("lam_t", DEPTH, 2, 32)
        lam_s = sb("lam_s", DEPTH, 2)
        lam_e = sb("lam_e", DEPTH, 2)
        neg_lam = sb("neg_lam", DEPTH)
        xc = sb("xc", DM)
        top_v = sb("top_v", 2, TOPK)
        top_i = sb("top_i", 2, TOPK, dt=u32)
        top_f = sb("top_f", 2, TOPK)
        sc2 = sb("sc2", 2, NKEYS)
        cand = sb("cand", TOPK, TOPK)
        cand2 = sb("cand2", TOPK, TOPK)
        best_v = sb("best_v", TOPK)
        best_p = sb("best_p", TOPK, dt=u32)
        pos_u = sb("pos_u", 2, TOPK, dt=u32)
        pos_f = sb("pos_f", 2, TOPK)
        hot = sb("hot", 2 * TOPK, TOPK)
        ij = sb("ij", 2, TOPK)
        idx = sb("idx", 2, TOPK, dt=u32)
        neg_best = sb("neg_best", 1)
        gate_e = sb("gate_e", TOPK)
        gate_s = sb("gate_s", 2)
        gate = sb("gate", 2, TOPK)
        hdot = sb("hdot", 2, CH)
        gel = sb("gel", 2, CH)
        amp = sb("amp", 2, CH)
        diag = sb("diag", NDIAG, P)

        bank = [ctx.enter_context(nc.psum_tensor(f"bank{i}", [P, 512], f32)) for i in range(BANKS)]
        ysum = ctx.enter_context(nc.psum_tensor("ysum", [P, DM], f32))

        s_const = sem("s_const")
        s_late = sem("s_late")
        s_xin = sem("s_xin")
        s_w = [sem(f"s_w{i}") for i in range(WS)]
        s_ready = sem("s_ready")
        s_done = {"act": sem("s_done_act"), "dve": sem("s_done_dve")}
        s_prep = sem("s_prep")
        s_lsum = sem("s_lsum")
        s_lexp = sem("s_lexp")
        s_lam = sem("s_lam")
        s_sd = sem("s_sd")
        s_xn = sem("s_xn")
        s_sq = sem("s_sq")
        s_nrm = sem("s_nrm")
        s_pd = sem("s_pd")
        s_cv = sem("s_cv")
        s_nb = sem("s_nb")
        s_ex = sem("s_ex")
        s_pw = sem("s_pw")
        s_g = [sem(f"s_g{i}") for i in range(SLOTS)]
        s_idx = sem("s_idx")
        s_gm = sem("s_gm")
        s_ge = sem("s_ge")
        s_h = sem("s_h")
        s_gl = sem("s_gl")
        s_gate = sem("s_gate")
        s_a = sem("s_a")
        s_dg = sem("s_dg")
        s_yc = sem("s_yc")
        s_x = sem("s_x")
        s_chain = sem("s_chain")
        s_out = sem("s_out")

        def ready(eng, m, name):
            eng.wait_ge(s_ready, m * NJOBS + JOB_AT[name] + 1)

        def done(eng, m, name):
            by = JOB_BY[name]
            eng.wait_ge(s_done[by], m * JOBS_OF[by] + JOB_NTH[name])

        def bank_of(m, name):
            return bank[(m * NJOBS + JOB_AT[name]) % BANKS]

        ident = cc[:, CC_ID:CC_ID + P]
        ones64 = cc[:, CC_O64:CC_O64 + P]
        ones32 = cc[:, CC_O32:CC_O32 + P]
        eps = cc[:, CC_EPS:CC_EPS + 1]
        CONSTS, LATE = 16 * 2, 16 * 5

        def zcol(layer, first):
            return small[:, layer, first:first + 1]

        def z_home(i, half):
            c = half * HALF
            if i == ZKB:
                return kB[:, c:c + HALF]
            if i in ZKD:
                return kD[:, i - ZKD[0], c:c + HALF]
            if i in ZP:
                return pT[:, i - ZP[0], PAD + c:PAD + c + HALF]
            order = ZQB + ZQD + ZH + ZG + ZC
            return zt[:, order.index(i), :]

        def head_start(mixer):
            for _ in range(SLICES - TAIL):
                next(mixer)
            return mixer

        def interleave(mixers, slices, peer, slices_first=False):
            ran = 0
            rest = chain_of(*mixers)
            for c in range(CHUNKS):
                if not slices_first:
                    next(peer)
                while ran < slices and ran * (CHUNKS - 2) < (c + 1) * slices:
                    next(rest)
                    ran += 1
                if slices_first:
                    next(peer)
            for _ in peer:
                pass
            for _ in rest:
                pass

        block = ctx.enter_context(nc.Block())

        @block.sync
        def _(sp):
            x_t = x_d.rearrange("(t p) d -> p t d", p=P)
            sp.dma_start(x[:, 0:TT, :], x_t[:, 0:TT, :]).then_inc(s_xin, 16)
            sp.dma_start(cc[:, :], consts_d).then_inc(s_const, 16)
            sp.dma_start(small[:, :, :], small_d).then_inc(s_const, 16)

            def load_w(n):
                m, b = divmod(n, WBLOCKS)
                if n >= WS:
                    pm, pb = divmod(n - WS, WBLOCKS)
                    ready(sp, pm, W_JOB[pb])
                sp.dma_start(w[:, n % WS, :, :], wall_d[m // 2, b]).then_inc(s_w[n % WS], 16)

            for n in range(WS):
                load_w(n)
            sp.dma_start(wpool[:, :, :, :], wpool_d).then_inc(s_late, 16)
            sp.dma_start(skt[:, :, :, :], skt_d).then_inc(s_late, 16)
            for layer in range(DEPTH):
                sp.dma_start(g2b[:, layer, :], g2b_d[layer]).then_inc(s_late, 16)
            sp.dma_start(x[:, TT:, :], x_t[:, TT:, :]).then_inc(s_late, 16)
            for n in range(WS, NBLK * WBLOCKS):
                load_w(n)
            first = SEQ // P * (DEPTH - 1)
            for t in range(SEQ // P):
                sp.wait_ge(s_x, first + t + 1)
                sp.dma_start(out_d[t * P:(t + 1) * P, :], x[:, t, :]).then_inc(s_out, 16)
            sp.wait_ge(s_out, 16 * (SEQ // P))

        @block.gpsimd
        def _(pool):
            for m in range(NBLK):
                for head in range(TT * HEADS):
                    g = m * TT * HEADS + head
                    pool.wait_ge(s_idx, g + 1)
                    for k in range(TOPK):
                        n = g * TOPK + k
                        if n >= SLOTS:
                            pool.wait_ge(s_yc, n - SLOTS + 1)
                        pool.indirect_dma_start(
                            gather[:, n % SLOTS, :], None, uv_d[m // 2],
                            bass.IndirectOffsetOnAxis(ap=idx[:, g % 2, k:k + 1], axis=0)
                        ).then_inc(s_g[n % SLOTS], 16)

        def mixer_pe(pe, m):
            layer, half = divmod(m, 2)
            t0 = half * TT

            def start(name):
                n = m * NJOBS + JOB_AT[name]
                if n >= BANKS:
                    pm, pj = divmod(n - BANKS, NJOBS)
                    done(pe, pm, JOBS[pj][0])
                return bank_of(m, name)

            def weights(b):
                n = m * WBLOCKS + b
                pe.wait_ge(s_w[n % WS], 16 * (n // WS + 1))
                return w[:, n % WS, :, :]

            def transposes(kind, which):
                for t in range(TT):
                    pe.wait_ge(s_xn, 4 * m + which + t + 1)
                    for h in range(2):
                        ps = start((kind, t, h))
                        for k in range(4):
                            d = 4 * h + k
                            mm = nc.tensor.transpose(ps[:, k * P:(k + 1) * P], xn[:, t, d * P:(d + 1) * P], ident)
                        mm.then_inc(s_ready, 1)
                    yield

            def project(name, b):
                wt = weights(b)
                ps = start(name)
                for d in range(KD):
                    mm = nc.tensor.matmul(ps[:, 0:HALF], wt[:, d, :], xnT[:, d, :], start=d == 0, stop=d == KD - 1)
                mm.then_inc(s_ready, 1)

            if m == 0:
                pe.wait_ge(s_const, CONSTS)
            yield from transposes("xT", 0)
            done(pe, m, ("xT", TT - 1, 1))
            for i in range(NORMED + NV):
                if i < NORMED:
                    project(("z", i), i)
                else:
                    wt = weights(i)
                    ps = start(("v", i - NORMED))
                    for t in range(TT):
                        for d in range(KD):
                            mm = nc.tensor.matmul(ps[:, t * P:(t + 1) * P], xnT[:, d, t * P:(t + 1) * P], wt[:, d, :],
                                                  start=d == 0, stop=d == KD - 1)
                    mm.then_inc(s_ready, 1)
                if 0 < i <= NORMED:
                    ps = start(("n", i - 1))
                    pe.wait_ge(s_sq, 15 * m + i)
                    nc.tensor.matmul(ps[:, 0:HALF], ones64 if i - 1 <= ZKB else ones32, sq[:, (15 * m + i - 1) % 2, :],
                                     start=True, stop=True).then_inc(s_ready, 1)
                yield
            for i in ZP:
                project(("z", i), NV + i)
                yield

            def attn_scores(a):
                swa, t, h, k0 = item(a, t0)
                tq, keys = (t - t0) * P, slice(k0 * P, (t + 1) * P)
                for mp in range(1 if swa else 2):
                    ps = start(("s", a, mp))
                    if swa:
                        rows = slice(64 * (h // 2), 64 * (h // 2) + 64)
                        q, k = zt[rows, h % 2, tq:tq + P], kB[rows, keys]
                    else:
                        row = 64 * (h % 2) + 32 * mp
                        rows = slice(row, row + 32)
                        q, k = zt[rows, 2 + h // 2, tq:tq + P], kD[rows, h // 2, keys]
                    nc.tensor.matmul(ps[:, 0:(t + 1 - k0) * P], q, k, start=True, stop=True).then_inc(s_ready, 1)

            pe.wait_ge(s_nrm, 15 * m + NORMED)
            attn_scores(0)
            attn_scores(1)
            yield
            for a in range(ITEMS + 1):
                if a < ITEMS:
                    swa, t, h, k0 = item(a, t0)
                    ps = start(("t", a))
                    pe.wait_ge(s_pw, ITEMS * m + a + 1)
                    for b in range(t + 1 - k0):
                        mm = nc.tensor.transpose(ps[:, b * P:(b + 1) * P], sc[:, a % 2, 0, b * P:(b + 1) * P], ident)
                    mm.then_inc(s_ready, 1)
                    if a + 2 < ITEMS:
                        attn_scores(a + 2)
                if a:
                    swa, t, h, k0 = item(a - 1, t0)
                    ps = start(("o", a - 1))
                    done(pe, m, ("t", a - 1))
                    col = (h // 2) * 64 if swa else P + h * 64
                    rows = slice(64 * (h % 2), 64 * (h % 2) + 64)
                    n = t + 1 - k0
                    for b in range(n):
                        mm = nc.tensor.matmul(ps[rows, 0:P], vAll[:, k0 + b, col:col + 64],
                                              pt[:, (a - 1) % 2, b * P:(b + 1) * P], start=b == 0, stop=b == n - 1)
                    mm.then_inc(s_ready, 1)
                if a < NLATE:
                    project(("z", ZH[0] + a), NV + ZH[0] + a)
                yield
            if m == 0:
                pe.wait_ge(s_late, LATE)
            for j in range(2):
                ps = start(("pool", j))
                pe.wait_ge(s_pd, 2 * m + j + 1)
                nc.tensor.matmul(ps[:, 0:HALF], wpool[:, layer, j, :], pd[:, j, :], start=True, stop=True)\
                    .then_inc(s_ready, 1)
            yield
            for n in range(8):
                ps = start(("y", n))
                pe.wait_ge(s_sq, 15 * m + NORMED + n + 1)
                nc.tensor.matmul(ps[:, 0:HALF], ones64, sq[:, (15 * m + NORMED + n) % 2, :], start=True, stop=True)\
                    .then_inc(s_ready, 1)
                yield
            pe.wait_ge(s_nrm, 15 * m + 15)
            for i in range(8):
                wt = weights(NZ + NV + i)
                ps = start(("out", i))
                for t in range(TT):
                    for c in range(8):
                        mm = nc.tensor.matmul(ps[:, t * P:(t + 1) * P], yT[:, c, t * P:(t + 1) * P], wt[:, c, :],
                                              start=c == 0, stop=c == 7)
                mm.then_inc(s_ready, 1)
                yield
            yield from transposes("x2T", 2)
            done(pe, m, ("x2T", TT - 1, 1))
            def key_scores(t, g):
                ps = start(("sk", t, g))
                done(pe, m, ("q", 4 * g + 3))
                for k in range(4):
                    hc = 4 * g + k
                    mm = nc.tensor.matmul(ps[:, k * P:(k + 1) * P], qT[:, hc, t * P:(t + 1) * P],
                                          skt[:, layer, hc % 2, :], start=True, stop=True)
                mm.then_inc(s_ready, 1)

            for i in range(16):
                project(("q", i), NZ + NV + 8 + i)
                yield
                if i % 4 == 3:
                    key_scores(0, i // 4)
                    yield
            for g in range(4):
                key_scores(1, g)
                yield

        def chunk_pe(pe, c):
            for j in range(CH):
                n = c * CH + j
                k = n % (HEADS * TOPK)
                if k == 0 and n:
                    pe.wait_ge(s_x, n // (HEADS * TOPK))
                pe.wait_ge(s_dg, n + 1)
                for hf in range(2):
                    mm = nc.tensor.matmul(ysum[:, hf * 512:(hf + 1) * 512], diag[:, n % NDIAG, :],
                                          gather[:, n % SLOTS, DM + hf * 512:DM + (hf + 1) * 512],
                                          start=k == 0, stop=k == HEADS * TOPK - 1)
                mm.then_inc(s_yc, 1)

        def peer_pe(pe, m):
            for c in range(CHUNKS):
                chunk_pe(pe, m * CHUNKS + c)
                yield

        @block.tensor
        def _(pe):
            first = head_start(mixer_pe(pe, 0))
            for m in range(NBLK):
                mixers = [mixer_pe(pe, m + 1)] if m + 1 < NBLK else []
                interleave([first] * (m == 0) + mixers, TAIL * (m == 0) + SLICES * len(mixers), peer_pe(pe, m), slices_first=True)

        def mixer_act(act, m):
            layer, half = divmod(m, 2)
            t0 = half * TT
            mean = 1.0 / DM

            def x_rms(which):
                for t in range(TT):
                    nc.scalar.activation(xn[:, t, :], x[:, t0 + t, :], ACT.Square, accum_out=ss[:, which + t:which + t + 1])\
                        .then_inc(s_actc, 1)
                    actc[0] += 1
                    act.wait_ge(s_actc, actc[0])
                    nc.scalar.activation(sdv[:, which + t:which + t + 1], ss[:, which + t:which + t + 1], ACT.Sqrt,
                                         bias=eps, scale=mean).then_inc(s_sd, 1)
                    yield

            def square(n, src):
                nn = 15 * m + n
                if nn >= 2:
                    pm, pn = divmod(nn - 2, 15)
                    ready(act, pm, ("n", pn) if pn < NORMED else ("y", pn - NORMED))
                nc.scalar.activation(sq[:, nn % 2, :], src, ACT.Square).then_inc(s_sq, 1)

            def root(name, n, width):
                nn = 15 * m + n
                ready(act, m, name)
                if nn >= 2:
                    act.wait_ge(s_nrm, nn - 1)
                nc.scalar.activation(sd[:, nn % 2, :], bank_of(m, name)[:, 0:HALF], ACT.Sqrt, bias=eps,
                                     scale=1.0 / width).then_inc(s_done["act"], 1)

            def empty(name, out, in_):
                ready(act, m, name)
                nc.scalar.activation(out, in_, ACT.Copy).then_inc(s_done["act"], 1)

            if m == 0:
                act.wait_ge(s_xin, 16)
                act.wait_ge(s_const, CONSTS)
            elif m == 1:
                act.wait_ge(s_late, LATE)
            elif layer:
                act.wait_ge(s_x, 2 * m - 2)
            if m:
                ready(act, m - 1, ("x2T", TT - 1, 1))
            yield from x_rms(0)
            for i in range(NORMED + NV):
                if i < NORMED:
                    empty(("z", i), z_home(i, half), bank_of(m, ("z", i))[:, 0:HALF])
                    done(act, m, ("z", i))
                    square(i, z_home(i, half))
                else:
                    empty(("v", i - NORMED), vAll[:, t0:t0 + TT, (i - NORMED) * P:(i - NORMED + 1) * P],
                          bank_of(m, ("v", i - NORMED))[:, 0:HALF].rearrange("p (t c) -> p t c", t=TT))
                if 0 < i <= NORMED:
                    root(("n", i - 1), i - 1, 64 if i - 1 <= ZKB else 32)
                yield
            for i in ZP:
                empty(("z", i), z_home(i, half), bank_of(m, ("z", i))[:, 0:HALF])
                yield

            def attn_exp(a):
                swa, t, h, k0 = item(a, t0)
                s, cols = a % 2, (t + 1 - k0) * P
                act.wait_ge(s_nb, ITEMS * m + a + 1)
                scale = (64 ** -0.5) * slope(h) if swa else (32 ** -0.5) * slope(4 + h)
                for mp in range(1 if swa else 2):
                    e = nc.scalar.activation(sc[:, s, mp, 0:cols], sc[:, s, mp, 0:cols], ACT.Exp,
                                             bias=st[:, s, 2 + mp:3 + mp], scale=scale,
                                             accum_out=st[:, s, 4 + mp:5 + mp])
                if swa:
                    e = nc.scalar.activation(st[:, s, 6:7], small[:, layer, SP_SINK + h:SP_SINK + h + 1], ACT.Exp,
                                             bias=st[:, s, 2:3])
                e.then_inc(s_ex, 1)

            attn_exp(0)
            yield
            for a in range(ITEMS + 1):
                if a < ITEMS:
                    swa, t, h, k0 = item(a, t0)
                    cols = (t + 1 - k0) * P
                    if a + 1 < ITEMS:
                        attn_exp(a + 1)
                    ready(act, m, ("t", a))
                    nc.scalar.activation(pt[:, a % 2, 0:cols], bank_of(m, ("t", a))[:, 0:cols], ACT.Copy)\
                        .then_inc(s_done["act"], 1)
                if a:
                    swa, t, h, k0 = item(a - 1, t0)
                    rows = slice(64 * (h % 2), 64 * (h % 2) + 64)
                    empty(("o", a - 1), yT[rows, (2 if swa else 6) + h // 2, (t - t0) * P:(t - t0 + 1) * P],
                          bank_of(m, ("o", a - 1))[rows, 0:P])
                if a < NLATE:
                    i = ZH[0] + a
                    empty(("z", i), z_home(i, half), bank_of(m, ("z", i))[:, 0:HALF])
                yield
            for j in range(2):
                empty(("pool", j), yT[:, j, :], bank_of(m, ("pool", j))[:, 0:HALF])
            yield
            act.wait_ge(s_cv, 2 * m + 2)
            done(act, m, ("pool", 1))
            for n in range(8):
                if n == 0:
                    square(NORMED, yT[:, YORDER[0], :])
                if n + 1 < 8:
                    square(NORMED + n + 1, yT[:, YORDER[n + 1], :])
                root(("y", n), NORMED + n, 64)
                yield
            for i in range(8):
                yield
            done(act, m, ("out", 7))
            yield from x_rms(2)
            def key_scores(t, g):
                if m:
                    act.wait_ge(s_idx, TT * HEADS * (m - 1) + HEADS * t + 2 * g + 2)
                empty(("sk", t, g), scores[:, t, 4 * g:4 * g + 4, :],
                      bank_of(m, ("sk", t, g))[:, :].rearrange("p (c k) -> p c k", c=4))

            for i in range(16):
                empty(("q", i), qT[:, i, :], bank_of(m, ("q", i))[:, 0:HALF])
                yield
                if i % 4 == 3:
                    key_scores(0, i // 4)
                    yield
            for g in range(4):
                key_scores(1, g)
                yield

        def gate_exp(act, g):
            act.wait_ge(s_gm, g + 1)
            nc.scalar.activation(gate_e[:, :], best_v[:, :], ACT.Exp, bias=neg_best[:, :],
                                 accum_out=gate_s[:, 0:1]).then_inc(s_ge, 1)

        def diagonals(act, c):
            act.wait_ge(s_h, c + 1)
            nc.scalar.activation(gel[:, c % 2, :], hdot[:, c % 2, :], ACT.Gelu).then_inc(s_gl, 1)
            act.wait_ge(s_gl, c + 1)
            if c % 4 == 0:
                act.wait_ge(s_gate, c // 4 + 1)
            for j in range(CH):
                k = c % 4 * CH + j
                nc.scalar.activation(amp[:, c % 2, j:j + 1], gel[:, c % 2, j:j + 1], ACT.Copy,
                                     scale=gate[:, c // 4 % 2, k:k + 1]).then_inc(s_a, 1)
            for j in range(CH):
                n = c * CH + j
                act.wait_ge(s_a, n + 1)
                if n >= NDIAG:
                    act.wait_ge(s_yc, n - NDIAG + 1)
                nc.scalar.activation(diag[:, n % NDIAG, :], ident, ACT.Copy, scale=amp[:, c % 2, j:j + 1]).then_inc(s_dg, 1)

        def peer_act(act, m):
            for c in range(CHUNKS):
                diagonals(act, m * CHUNKS + c)
                g = m * TT * HEADS + c // 4 + 1
                if c % 4 == 1 and g < NBLK * TT * HEADS:
                    gate_exp(act, g)
                yield

        actc = [0]
        s_actc = sem("s_actc")

        @block.scalar
        def _(act):
            act.wait_ge(s_lsum, 1)
            nc.scalar.activation(lam_e[:, :, :], lam_s[:, :, :], ACT.Exp).then_inc(s_lexp, 1)
            first = head_start(mixer_act(act, 0))
            gate_exp(act, 0)
            for m in range(NBLK):
                mixers = [mixer_act(act, m + 1)] if m + 1 < NBLK else []
                interleave([first] * (m == 0) + mixers, TAIL * (m == 0) + SLICES * len(mixers), peer_act(act, m))

        V = nc.vector
        chained = [0]

        def chain(dve, ins):
            chained[0] += 1
            ins.then_inc(s_chain, 1)
            dve.wait_ge(s_chain, chained[0])

        def mixer_dve(dve, m):
            layer, half = divmod(m, 2)
            t0 = half * TT

            def normalise_x(which, kind, gain, rr):
                for t in range(TT):
                    dve.wait_ge(s_sd, 4 * m + which + t + 1)
                    chain(dve, V.reciprocal(rr[t], sdv[:, which + t:which + t + 1]))
                    V.tensor_scalar(xn[:, t, :], x[:, t0 + t, :], rr[t], None, ALU.mult).then_inc(s_xn, 1)
                    for h in range(2):
                        ready(dve, m, (kind, t, h))
                        V.tensor_tensor(
                            xnT[:, 4 * h:4 * h + 4, t * P:(t + 1) * P],
                            bank_of(m, (kind, t, h))[:, :].rearrange("p (k c) -> p k c", k=4),
                            small[:, layer, gain + 4 * h:gain + 4 * h + 4].unsqueeze(2).to_broadcast([P, 4, P]),
                            ALU.mult).then_inc(s_done["dve"], 1)
                    yield

            def normalise(n, tile, gain):
                nn = 15 * m + n
                done(dve, m, ("n", n) if n < NORMED else ("y", n - NORMED))
                chain(dve, V.reciprocal(sd[:, nn % 2, :], sd[:, nn % 2, :]))
                V.scalar_tensor_tensor(tile, tile, gain, sd[:, nn % 2, :], ALU.mult, ALU.mult).then_inc(s_nrm, 1)

            if m == 0:
                dve.wait_ge(s_xin, 16)
            elif m == 1:
                dve.wait_ge(s_late, LATE)
            elif layer:
                dve.wait_ge(s_x, 2 * m - 2)
            yield from normalise_x(0, "xT", SP_G1, [r1[:, t:t + 1] for t in range(TT)])
            for i in range(NORMED + NV + 2):
                if 0 < i <= NORMED:
                    normalise(i - 1, z_home(i - 1, half), zcol(layer, SP_QKG + i - 1))
                yield

            def attn_bias(a):
                swa, t, h, k0 = item(a, t0)
                s, cols = a % 2, (t + 1 - k0) * P
                scale = (64 ** -0.5) * slope(h) if swa else (32 ** -0.5) * slope(4 + h)
                for mp in range(1 if swa else 2):
                    ready(dve, m, ("s", a, mp))
                    bias = cc[:, CC_DB + 256 - cols:CC_DB + 256] if swa else cc[:, CC_DD + 512 - cols:CC_DD + 512]
                    V.tensor_tensor_reduce(out=sc[:, s, mp, 0:cols], in0=bank_of(m, ("s", a, mp))[:, 0:cols], in1=bias,
                                           scale=1.0, scalar=-BIG, op0=ALU.add, op1=ALU.max,
                                           accum_out=st[:, s, mp:mp + 1]).then_inc(s_done["dve"], 1)
                done(dve, m, ("s", a, 0 if swa else 1))
                if swa:
                    chain(dve, V.tensor_scalar(st[:, s, 0:1], st[:, s, 0:1], scale, None, ALU.mult))
                    chain(dve, V.tensor_tensor(st[:, s, 0:1], st[:, s, 0:1],
                                               small[:, layer, SP_SINK + h:SP_SINK + h + 1], ALU.max))
                    V.tensor_scalar(st[:, s, 2:3], st[:, s, 0:1], -1.0, None, ALU.mult).then_inc(s_nb, 1)
                else:
                    V.tensor_scalar(st[:, s, 2:4], st[:, s, 0:2], -scale, None, ALU.mult).then_inc(s_nb, 1)

            def attn_weights(a):
                swa, t, h, k0 = item(a, t0)
                s, cols = a % 2, (t + 1 - k0) * P
                dve.wait_ge(s_ex, ITEMS * m + a + 1)
                if swa:
                    chain(dve, V.tensor_tensor(st[:, s, 7:8], st[:, s, 4:5], st[:, s, 6:7], ALU.add))
                    chain(dve, V.reciprocal(st[:, s, 8:9], st[:, s, 7:8]))
                    V.tensor_scalar(sc[:, s, 0, 0:cols], sc[:, s, 0, 0:cols], st[:, s, 8:9], None, ALU.mult)\
                        .then_inc(s_pw, 1)
                else:
                    chain(dve, V.reciprocal(st[:, s, 8:10], st[:, s, 4:6]))
                    chain(dve, V.tensor_tensor(st[:, s, 10:11], st[:, s, 9:10], neg_lam[:, layer:layer + 1], ALU.mult))
                    chain(dve, V.tensor_scalar(sc[:, s, 0, 0:cols], sc[:, s, 0, 0:cols], st[:, s, 8:9], None, ALU.mult))
                    V.scalar_tensor_tensor(sc[:, s, 0, 0:cols], sc[:, s, 1, 0:cols], st[:, s, 10:11],
                                           sc[:, s, 0, 0:cols], ALU.mult, ALU.add).then_inc(s_pw, 1)

            c0 = half * HALF
            done(dve, m, ("z", ZP[1]))
            for j in range(2):
                src = pT[:, j, c0:c0 + PAD + HALF]
                for lv in range(2 if j == 0 else 4):
                    sh = 1 << lv
                    lo = 2 * sh - 1
                    chain(dve, V.tensor_tensor(pool_sum[:, lv, lo:PAD + HALF], src[:, lo:PAD + HALF],
                                               src[:, lo - sh:PAD + HALF - sh], ALU.add))
                    src = pool_sum[:, lv, :]
                for part in range(2):
                    rows = slice(64 * part, 64 * part + 64)
                    lv = 2 * j + part
                    if half == 0:
                        chain(dve, V.tensor_tensor(pool_sum[rows, lv, PAD:2 * PAD], pool_sum[rows, lv, PAD:2 * PAD],
                                                   cc[rows, CC_CORR + PAD * j:CC_CORR + PAD * (j + 1)], ALU.mult))
                    e = V.scalar_tensor_tensor(pd[rows, j, :], pool_sum[rows, lv, PAD:PAD + HALF],
                                               cc[rows, CC_INVW + j:CC_INVW + j + 1],
                                               pT[rows, j, PAD + c0:PAD + c0 + HALF], ALU.mult, ALU.subtract)
                    if part:
                        e.then_inc(s_pd, 1)
                    else:
                        chain(dve, e)
            dve.wait_ge(s_pd, 2 * m + 2)
            attn_bias(0)
            attn_bias(1)
            attn_weights(0)
            yield
            for a in range(ITEMS + 1):
                if a < ITEMS:
                    if a + 1 < ITEMS:
                        attn_weights(a + 1)
                    if a + 2 < ITEMS:
                        ready(dve, m, ("t", a))
                        attn_bias(a + 2)
                yield
            done(dve, m, ("z", NZ - 1))
            for j in range(2):
                hh, gg, cg = (z_home(z[j], half) for z in (ZH, ZG, ZC))
                yc = yT[:, 4 + j, :]
                chain(dve, V.tensor_tensor(cT[:, j, PAD + c0:PAD + c0 + HALF], cg, hh, ALU.mult))
                tap = [cT[:, j, PAD + c0 - 2 + k:PAD + c0 - 2 + k + HALF] for k in range(3)]
                wc = [zcol(layer, SP_CONV + 2 * k + j) for k in range(3)]
                chain(dve, V.tensor_scalar(yc, tap[0], wc[0], None, ALU.mult))
                chain(dve, V.scalar_tensor_tensor(yc, tap[1], wc[1], yc, ALU.mult, ALU.add))
                chain(dve, V.scalar_tensor_tensor(yc, tap[2], wc[2], yc, ALU.mult, ALU.add))
                V.tensor_tensor(yc, yc, gg, ALU.mult).then_inc(s_cv, 1)
            yield
            for n in range(8):
                y = YORDER[n]
                normalise(NORMED + n, yT[:, y, :], zcol(layer, SP_OG + y))
                yield
            for i in range(8):
                ready(dve, m, ("out", i))
                V.tensor_tensor(x[:, t0:t0 + TT, i * P:(i + 1) * P],
                                bank_of(m, ("out", i))[:, 0:HALF].rearrange("p (t c) -> p t c", t=TT),
                                x[:, t0:t0 + TT, i * P:(i + 1) * P], ALU.add).then_inc(s_done["dve"], 1)
                yield
            done(dve, m, ("out", 7))
            yield from normalise_x(2, "x2T", SP_G2, [r2[:, t0 + t:t0 + t + 1] for t in range(TT)])
            for i in range(16 + 4 * TT):
                yield

        def top16(dve, vals, spare, tv, ti):
            chain(dve, V.max(tv[:, 0:8], vals))
            V.max_index(ti[:, 0:8], tv[:, 0:8], vals)
            chain(dve, V.match_replace(spare, tv[:, 0:8], vals, -BIG))
            chain(dve, V.max(tv[:, 8:16], spare))
            chain(dve, V.max_index(ti[:, 8:16], tv[:, 8:16], spare))

        def route_keys(dve, m, head):
            t, h = divmod(head, HEADS)
            done(dve, m, ("sk", t, h // 2))
            for c in range(2):
                top16(dve, scores[:, t, 2 * h + c, :], sc2[:, c, :], top_v[:, c, :], top_i[:, c, :])
            V.tensor_copy(top_f[:, :, :], top_i[:, :, :])
            chain(dve, V.tensor_tensor(cand[:, :, :], top_v[:, 0, :].unsqueeze(2).to_broadcast([P, TOPK, TOPK]),
                                       top_v[:, 1, :].unsqueeze(1).to_broadcast([P, TOPK, TOPK]), ALU.add))

        def route_experts(dve, m, head):
            g = m * TT * HEADS + head
            flat = lambda c: c[:, :, :].rearrange("p a b -> p (a b)")
            if g:
                dve.wait_ge(s_ge, g)
            top16(dve, flat(cand), flat(cand2), best_v, best_p)
            V.tensor_scalar(neg_best[:, :], best_v[:, 0:1], -1.0, None, ALU.mult).then_inc(s_gm, 1)
            V.tensor_scalar(pos_u[:, 0, :], best_p[:, :], 4, None, ALU.logical_shift_right)
            chain(dve, V.tensor_scalar(pos_u[:, 1, :], best_p[:, :], 15, None, ALU.bitwise_and))
            chain(dve, V.tensor_copy(pos_f[:, :, :], pos_u[:, :, :]))
            both = [P, 2 * TOPK, TOPK]
            chain(dve, V.tensor_tensor(
                hot[:, :, :], pos_f[:, :, :].rearrange("p c k -> p (c k)").unsqueeze(2).to_broadcast(both),
                cc[:, CC_IOTA:CC_IOTA + TOPK].unsqueeze(1).to_broadcast(both), ALU.is_equal))
            hot4 = hot[:, :, :].rearrange("p (c k) a -> p c k a", c=2)
            chain(dve, V.tensor_tensor(hot4, hot4, top_f[:, :, :].unsqueeze(2).to_broadcast([P, 2, TOPK, TOPK]), ALU.mult))
            chain(dve, V.tensor_reduce(ij[:, :, :].rearrange("p c k -> p (c k)"), hot[:, :, :], AX, ALU.add))
            V.scalar_tensor_tensor(idx[:, g % 2, :], ij[:, 0, :], float(NKEYS), ij[:, 1, :], ALU.mult, ALU.add)\
                .then_inc(s_idx, 1)

        def route_gate(dve, m, head):
            g = m * TT * HEADS + head
            dve.wait_ge(s_ge, g + 1)
            if g >= 2:
                dve.wait_ge(s_a, (g - 1) * TOPK)
            chain(dve, V.reciprocal(gate_s[:, 1:2], gate_s[:, 0:1]))
            V.tensor_scalar(gate[:, g % 2, :], gate_e[:, :], gate_s[:, 1:2], None, ALU.mult).then_inc(s_gate, 1)

        def peer_dve(dve, m):
            layer = m // 2
            def add_tile(tg):
                dve.wait_ge(s_yc, (tg + 1) * HEADS * TOPK)
                t = tg % (SEQ // P)
                V.tensor_tensor(x[:, t, :], ysum[:, :], x[:, t, :], ALU.add).then_inc(s_x, 1)

            per_tile = CHUNKS // TT
            for c in range(CHUNKS):
                cg = m * CHUNKS + c
                t = (m % 2) * TT + c // per_tile
                head = c // 4
                if c % per_tile == 0:
                    if c == 0:
                        done(dve, m, ("out", 7))
                    chain(dve, V.scalar_tensor_tensor(xc[:, :], x[:, t, :], r2[:, t:t + 1], g2b[:, layer, :],
                                                      ALU.mult, ALU.mult))
                if cg >= 2:
                    dve.wait_ge(s_gl, cg - 1)
                for j in range(CH):
                    n = cg * CH + j
                    dve.wait_ge(s_g[n % SLOTS], 16 * (n // SLOTS + 1))
                    e = V.tensor_tensor_reduce(out=gather[:, n % SLOTS, 0:DM], in0=gather[:, n % SLOTS, 0:DM],
                                               in1=xc[:, :], scale=1.0, scalar=0.0, op0=ALU.mult, op1=ALU.add,
                                               accum_out=hdot[:, cg % 2, j:j + 1])
                    if j == CH - 1:
                        e.then_inc(s_h, 1)
                if c == per_tile:
                    add_tile(m * TT)
                nm, nh = divmod(m * TT * HEADS + head + 1, TT * HEADS)
                if nm < NBLK:
                    if c % 4 == 0:
                        route_keys(dve, nm, nh)
                    elif c % 4 == 1:
                        route_experts(dve, nm, nh)
                    elif c % 4 == 3:
                        route_gate(dve, nm, nh)
                yield
            add_tile(m * TT + 1)

        @block.vector
        def _(dve):
            V.memset(pT[:, :, 0:PAD], 0.0).then_inc(s_prep, 1)
            V.memset(cT[:, :, 0:PAD], 0.0).then_inc(s_prep, 1)
            dve.wait_ge(s_const, CONSTS)
            for layer in range(DEPTH):
                lam = small[:, layer, SP_LAM:SP_LAM + 128].rearrange("p (a b k) -> p a b k", a=2, b=2)
                chain(dve, V.tensor_tensor(lam_t[:, layer, :, :], lam[:, :, 0, :], lam[:, :, 1, :], ALU.mult))
                for n, i in enumerate(ZQB + ZQD):
                    gcol = zcol(layer, SP_QKG + i)
                    chain(dve, V.tensor_tensor(gcol, gcol, cc[:, CC_SLI + n:CC_SLI + n + 1], ALU.mult))
                og = small[:, layer, SP_OG + 6:SP_OG + 8]
                chain(dve, V.tensor_scalar(og, og, 1.0 - lam_init(layer), None, ALU.mult))
            V.tensor_reduce(lam_s[:, :, :], lam_t[:, :, :, :], AX, ALU.add).then_inc(s_lsum, 1)
            dve.wait_ge(s_lexp, 1)
            for layer in range(DEPTH):
                chain(dve, V.tensor_tensor(neg_lam[:, layer:layer + 1], lam_e[:, layer, 1:2], lam_e[:, layer, 0:1],
                                           ALU.subtract))
                chain(dve, V.tensor_scalar(neg_lam[:, layer:layer + 1], neg_lam[:, layer:layer + 1],
                                           -lam_init(layer), None, ALU.add))
            first = head_start(mixer_dve(dve, 0))
            route_keys(dve, 0, 0)
            route_experts(dve, 0, 0)
            route_gate(dve, 0, 0)
            for m in range(NBLK):
                mixers = [mixer_dve(dve, m + 1)] if m + 1 < NBLK else []
                interleave([first] * (m == 0) + mixers, TAIL * (m == 0) + SLICES * len(mixers), peer_dve(dve, m))


SLICES = 2 + NORMED + NV + 2 + 1 + ITEMS + 1 + 1 + 8 + 8 + 2 + 16 + 4 + 4
TAIL = 12 + 3 + 4


def columns():
    a, qb, kb, vb, h, b, c, qd, kd, vd = np.cumsum([0, 256, 256, 128, 128, 256, 256, 256, 256, 256])
    r = np.arange
    heads = lambda first, hs: np.concatenate([first + 64 * h + r(64) for h in hs])
    tiles = [heads(qb, (0, 2)), heads(qb, (1, 3)), kb + r(128), qd + r(128), qd + 128 + r(128),
             kd + r(128), kd + 128 + r(128), vb + r(128), vd + r(128), vd + 128 + r(128),
             a + r(128), a + 128 + r(128)]
    for first in (h, b, c):
        tiles += [first + r(128), first + 128 + r(128)]
    return np.concatenate(tiles)


def layout_weights(w_in, w_out, w_query):
    both = np.concatenate([w_in[:, :, columns()], w_out, w_query], axis=2)
    tiled = both.reshape(DEPTH, KD, P, WBLOCKS, P)
    return np.ascontiguousarray(tiled.transpose(0, 3, 2, 1, 4))


def layout_small(i):
    out = np.zeros((P, DEPTH, SP_N), np.float32)
    for l in range(DEPTH):
        s = out[:, l]
        s[:, SP_G1:SP_G1 + 8] = i["norm1_g"][l].reshape(8, P).T
        s[:, SP_G2:SP_G2 + 8] = i["norm2_g"][l].reshape(8, P).T
        s[:, SP_OG:SP_OG + 8] = i["out_norm_g"][l].reshape(8, P).T
        for n, name in enumerate(["swa_q_norm"] * 2 + ["swa_k_norm"] + ["diff_q_norm"] * 2 + ["diff_k_norm"] * 2):
            g = i[name][l]
            s[:, SP_QKG + n] = np.tile(g, P // g.size)
        for k in range(3):
            for j in range(2):
                s[:, SP_CONV + 2 * k + j] = i["conv_w"][l, k, j * P:(j + 1) * P]
        s[:, SP_SINK:SP_SINK + 4] = i["swa_sinks"][l][None]
        s[:, SP_LAM:SP_LAM + 128] = np.concatenate([i[n][l] for n in ("lam_q1", "lam_k1", "lam_q2", "lam_k2")])[None]
    return out


def layout_consts():
    c = np.zeros((P, CC_N), np.float32)
    q = np.arange(P)[:, None]
    c[:, CC_ID:CC_ID + P] = np.eye(P)
    c[:, CC_O64:CC_O64 + P] = q // 64 == np.arange(P)[None] // 64
    c[:, CC_O32:CC_O32 + P] = q // 32 == np.arange(P)[None] // 32
    dist = q + 128 - np.arange(256)[None]
    c[:, CC_DB:CC_DB + 256] = np.where((dist >= 0) & (dist < 128), -dist * math.sqrt(64), MASK)
    dist = q + 384 - np.arange(512)[None]
    c[:, CC_DD:CC_DD + 512] = np.where(dist >= 0, -dist * math.sqrt(32), MASK)
    c[:, CC_IOTA:CC_IOTA + TOPK] = np.arange(TOPK)[None]
    for j in range(2):
        for part in range(2):
            win = 2 ** (2 * j + part + 1)
            rows = slice(64 * part, 64 * part + 64)
            c[rows, CC_INVW + j] = 1.0 / win
            c[rows, CC_CORR + PAD * j:CC_CORR + PAD * (j + 1)] = win / np.minimum(np.arange(PAD) + 1, win)
    for rows, base in ((slice(0, 64), 0), (slice(64, 128), 1)):
        for g in range(2):
            c[rows, CC_SLI + g] = 1.0 / slope(2 * base + g)
            c[rows, CC_SLI + 2 + g] = 1.0 / slope(4 + 2 * g + base)
    c[:, CC_EPS] = EPS
    return c


def kernel(**inputs):
    import concourse.bacc as bacc
    from concourse.bass_utils import run_bass_kernel_spmd as run
    i = {k: np.asarray(v) for k, v in inputs.items()}
    wp = np.zeros((P, DEPTH, 2, P), np.float32)
    for l in range(DEPTH):
        for g in range(4):
            r = slice(64 * (g % 2), 64 * (g % 2) + 64)
            wp[r, l, g // 2, r] = i["w_pool"][l, g]
    arrays = {
        "x_in": np.ascontiguousarray(i["x"].reshape(SEQ, DM)),
        "weights": layout_weights(i["w_in"], i["w_out"], i["w_query"]),
        "small_in": layout_small(i),
        "consts_in": layout_consts(),
        "g2_rows": np.ascontiguousarray(np.broadcast_to(i["norm2_g"][:, None, :], (DEPTH, P, DM))),
        "wpool_in": wp,
        "keys_t": np.ascontiguousarray(i["sub_keys"].transpose(3, 0, 1, 2)),
    }
    for l in range(DEPTH):
        arrays[f"experts{l}"] = np.concatenate([i["peer_u"][l], i["peer_v"][l]], axis=1)
    nc = bacc.Bacc("TRN2", target_bir_lowering=False, num_devices=1)
    aps = [nc.dram_tensor(n, a.shape, mybir.dt.from_np(a.dtype), kind="ExternalInput").ap() for n, a in arrays.items()]
    out = nc.dram_tensor("y_out", (SEQ, DM), mybir.dt.float32, kind="ExternalOutput").ap()
    build(nc, *aps[:7], aps[7:], out)
    r = run(nc, [arrays], core_ids=[0])
    return r.results[0]["y_out"].reshape(1, SEQ, DM)
```

```python
import math
from contextlib import ExitStack
from itertools import chain as chain_of

import numpy as np
import concourse.bass as bass
from concourse import mybir

DEPTH, SEQ, DM = 2, 512, 1024
P = 128
HALF = 256
TT = HALF // P
NBLK = 2 * DEPTH
KD = DM // P
EPS = 1e-6
PAD = 16
HEADS, TOPK, NKEYS = 8, 16, 128
CH = 4
CHUNKS = HEADS * TT * TOPK // CH
SLOTS = 9
NDIAG = 4
WS = 4
BIG = 3.0e38
MASK = -1.0e30

ZQB, ZKB, ZQD, ZKD = (0, 1), 2, (3, 4), (5, 6)
NORMED = 7
ZP, ZH, ZG, ZC = (7, 8), (9, 12), (10, 13), (11, 14)
NZ = 15
NV = 3
AHEAD = (4, 2)
MEANS_AT, CONV_AT = (2, 4), (6, 8)
POOL_AT = 9
WBLOCKS = NZ + NV + 8 + 16
ITEMS = 16
YORDER = (4, 5, 0, 1, 2, 3, 6, 7)

SP_G1, SP_G2, SP_OG, SP_QKG, SP_CONV, SP_SINK, SP_LAM = 0, 8, 16, 24, 31, 37, 41
SP_N = SP_LAM + 128
CC_ID, CC_O64, CC_O32, CC_DB, CC_DD, CC_IOTA, CC_INVW, CC_CORR, CC_SLI, CC_EPS = (
    0, 128, 256, 384, 640, 1152, 1168, 1170, 1202, 1206)
CC_N = CC_EPS + 1


def slope(h):
    return 2.0 ** -(h + 1)


def lam_init(layer):
    return 0.8 - 0.6 * float(np.exp(-0.3 * layer))


def layout_jobs(half):
    jobs = [(("xT", t, h), "dve", None) for t in range(TT) for h in range(2)]
    for i in range(NORMED + NV):
        jobs.append((("z", i), "act", i) if i < NORMED else (("v", i - NORMED), "act", i))
        if 0 < i <= NORMED:
            jobs.append((("n", i - 1), "act", None))
    scores = lambda a: [(("s", a, k), "dve", None) for k in range(1 if a < 8 else 2)]
    ahead = AHEAD[half]
    for a in range(ahead):
        jobs += scores(a)
    for a in range(ITEMS + 1):
        if a < ITEMS:
            jobs.append((("t", a), "act", None))
            if a + ahead < ITEMS:
                jobs += scores(a + ahead)
        if a:
            jobs.append((("o", a - 1), "act", None))
        if a < NZ - NORMED:
            jobs.append((("z", NORMED + a), "act", NV + NORMED + a))
        if a == POOL_AT:
            jobs += [(("pool", j), "act", None) for j in range(2)]
        if a > POOL_AT:
            jobs.append((("y", a - POOL_AT - 1), "act", None))
    jobs += [(("y", i), "act", None) for i in range(ITEMS - POOL_AT, 8)]
    jobs += [(("out", i), "dve", NZ + NV + i) for i in range(8)]
    jobs += [(("x2T", t, h), "dve", None) for t in range(TT) for h in range(2)]
    for i in range(16):
        jobs.append((("q", i), "act", NZ + NV + 8 + i))
        if i % 2:
            jobs.append((("sk", 0, i // 2), "act", None))
    jobs += [(("sk", 1, h), "act", None) for h in range(HEADS)]
    return jobs


JOBS = [layout_jobs(half) for half in range(2)]
NJOBS = len(JOBS[0])
JOB_AT = [{name: n for n, (name, _, _) in enumerate(jobs)} for jobs in JOBS]
JOB_BY = {name: by for name, by, _ in JOBS[0]}
JOBS_OF = {by: sum(b == by for _, b, _ in JOBS[0]) for by in ("act", "dve")}
JOB_NTH = [{name: sum(b == by for _, b, _ in jobs[:n + 1]) for n, (name, by, _) in enumerate(jobs)} for jobs in JOBS]
W_JOB = {w: name for name, _, w in JOBS[0] if w is not None}
BANKS = 6



def work(half):
    return ([9, 6, 6] + [8] * (NORMED + NV) + [6] + [11] * 8 + [12 if half else 10] * (ITEMS - 7)
            + [10] * (8 - ITEMS + POOL_AT) + [8] * 8 + [9, 6, 6] + [8, 8, 2] * HEADS + [3] * 4)


SLICES = len(work(0))
TAIL = 3 * (HEADS - 1) + 4


def item(a, t0):
    swa = a < 8
    t, h = t0 + a % 8 // 4, a % 4
    return swa, t, h, (max(t - 1, 0) if swa else 0)


def build(nc, x_d, wall_d, small_d, consts_d, g2b_d, late_d, uv_d, out_d):
    f32, u32 = mybir.dt.float32, mybir.dt.uint32
    ALU, ACT, AX = mybir.AluOpType, mybir.ActivationFunctionType, mybir.AxisListType.X
    ctx = ExitStack()
    with ctx:
        def sb(name, *shape, dt=f32):
            return ctx.enter_context(nc.sbuf_tensor(name, [P, *shape], dt))

        def sem(name):
            return ctx.enter_context(nc.semaphore(name))

        x = sb("x", SEQ // P, DM)
        gather = sb("gather", SLOTS, 2 * DM)
        xnT = sb("xnT", KD, HALF)
        shared = sb("shared", 16 * HALF + 512)
        zt = shared[:, 0:10 * HALF].rearrange("p (i t) -> p i t", t=HALF)
        sc = [shared[:, 10 * HALF:10 * HALF + 2048].rearrange("p (s m k) -> p s m k", s=n, m=2) for n in AHEAD]
        qT = shared[:, 0:16 * HALF].rearrange("p (i t) -> p i t", t=HALF)
        kB = sb("kB", SEQ)
        kD = sb("kD", 2, SEQ)
        vAll = sb("vAll", SEQ // P, NV * P)
        pT = sb("pT", 2, PAD + SEQ)
        cT = sb("cT", 2, PAD + SEQ)
        yT = sb("yT", 8, HALF)
        pd = yT[:, 0:2, :]
        xn = yT[:, :, :].rearrange("p i t -> p (i t)").rearrange("p (t d) -> p t d", t=TT)
        scores = sb("scores", TT, 16, NKEYS)
        w = sb("w", WS, KD, P)
        small = sb("small", DEPTH, SP_N)
        cc = sb("cc", CC_N)
        g2b = sb("g2b", DM)
        late = sb("late", 4, P)
        wpool, skt = late[:, 0:2, :], late[:, 2:4, :]
        sq = sb("sq", 2, HALF)
        sd = sb("sd", 2, HALF)
        pt_all = sb("pt", 1024)
        pt = [pt_all[:, :].rearrange("p (s k) -> p s k", s=n) for n in AHEAD]
        ss = sb("ss", 4)
        sdv = sb("sdv", 4)
        r1 = sb("r1", TT)
        r2 = sb("r2", SEQ // P)
        st = sb("st", AHEAD[0], 12)
        lam_t = sb("lam_t", DEPTH, 2, 32)
        lam_s = sb("lam_s", DEPTH, 2)
        lam_e = sb("lam_e", DEPTH, 2)
        neg_lam = sb("neg_lam", DEPTH)
        xc = sb("xc", DM)
        top_v = sb("top_v", 2, TOPK)
        top_i = sb("top_i", 2, TOPK, dt=u32)
        top_f = sb("top_f", 2, TOPK)
        scratch = sb("scratch", 768)
        hot = scratch[:, 0:512].rearrange("p (k a) -> p k a", a=TOPK)
        sc2 = scratch[:, 512:768].rearrange("p (c k) -> p c k", c=2)
        pool_sum = scratch[:, 0:2 * (PAD + HALF)].rearrange("p (i t) -> p i t", i=2)
        cand = sb("cand", TOPK, TOPK)
        cand2 = sb("cand2", TOPK, TOPK)
        best_v = sb("best_v", TOPK)
        best_p = sb("best_p", TOPK, dt=u32)
        pos_u = sb("pos_u", 2, TOPK, dt=u32)
        pos_f = sb("pos_f", 2, TOPK)
        ij = sb("ij", 2, TOPK)
        idx = sb("idx", 2, TOPK, dt=u32)
        neg_best = sb("neg_best", 1)
        gate_e = sb("gate_e", TOPK)
        gate_s = sb("gate_s", 2)
        gate = sb("gate", 2, TOPK)
        hdot = sb("hdot", 2, CH)
        gel = sb("gel", 2, CH)
        amp = sb("amp", 2, CH)
        diag = sb("diag", NDIAG, P)

        bank = [ctx.enter_context(nc.psum_tensor(f"bank{i}", [P, 512], f32)) for i in range(BANKS)]
        ysum = ctx.enter_context(nc.psum_tensor("ysum", [P, DM], f32))

        s_const = sem("s_const")
        s_late = sem("s_late")
        s_g2b = sem("s_g2b")
        s_xin = [sem(f"s_xin{t}") for t in range(TT)]
        s_xrest = sem("s_xrest")
        s_w = [sem(f"s_w{i}") for i in range(WS)]
        s_ready = sem("s_ready")
        s_done = {"act": sem("s_done_act"), "dve": sem("s_done_dve")}
        s_prep = sem("s_prep")
        s_lsum = sem("s_lsum")
        s_lexp = sem("s_lexp")
        s_sd = sem("s_sd")
        s_xn = sem("s_xn")
        s_sq = sem("s_sq")
        s_nrm = sem("s_nrm")
        s_pd = sem("s_pd")
        s_cv = sem("s_cv")
        s_nb = sem("s_nb")
        s_ex = sem("s_ex")
        s_pw = sem("s_pw")
        s_g = [sem(f"s_g{i}") for i in range(SLOTS)]
        s_idx = sem("s_idx")
        s_gm = sem("s_gm")
        s_ge = sem("s_ge")
        s_h = sem("s_h")
        s_hlast = sem("s_hlast")
        s_gl = sem("s_gl")
        s_gate = sem("s_gate")
        s_a = sem("s_a")
        s_dg = sem("s_dg")
        s_yc = sem("s_yc")
        s_x = sem("s_x")
        s_chain = sem("s_chain")
        s_out = sem("s_out")

        def ready(eng, m, name):
            eng.wait_ge(s_ready, m * NJOBS + JOB_AT[m % 2][name] + 1)

        def done(eng, m, name):
            by = JOB_BY[name]
            eng.wait_ge(s_done[by], m * JOBS_OF[by] + JOB_NTH[m % 2][name])

        def bank_of(m, name):
            return bank[(m * NJOBS + JOB_AT[m % 2][name]) % BANKS]

        ident = cc[:, CC_ID:CC_ID + P]
        ones64 = cc[:, CC_O64:CC_O64 + P]
        ones32 = cc[:, CC_O32:CC_O32 + P]
        eps = cc[:, CC_EPS:CC_EPS + 1]
        CONSTS = 16 * 2

        def zcol(layer, first):
            return small[:, layer, first:first + 1]

        def z_home(i, half):
            c = half * HALF
            if i == ZKB:
                return kB[:, c:c + HALF]
            if i in ZKD:
                return kD[:, i - ZKD[0], c:c + HALF]
            if i in ZP:
                return pT[:, i - ZP[0], PAD + c:PAD + c + HALF]
            order = ZQB + ZQD + ZH + ZG + ZC
            return zt[:, order.index(i), :]

        def head_start(mixer, ran=0):
            for _ in range(SLICES - TAIL - ran):
                next(mixer)
            return mixer

        def interleave(m, mixer, peer, first, slices_first=False):
            slices = work((m + 1) % 2) if m + 1 < NBLK else []
            rest = mixer(m + 1) if m + 1 < NBLK else iter(())
            if m == 0:
                slices = [3] * 3 + work(0)[SLICES - TAIL + 3:] + slices
                rest = chain_of(first, rest)
            ran, spent, total = 0, 0, sum(slices)
            for c in range(CHUNKS):
                if not slices_first:
                    next(peer)
                while ran < len(slices) and spent * (CHUNKS - 2) < (c + 1) * total:
                    next(rest)
                    spent += slices[ran]
                    ran += 1
                if slices_first:
                    next(peer)
            for _ in peer:
                pass
            for _ in rest:
                pass

        block = ctx.enter_context(nc.Block())

        @block.sync
        def _(sp):
            x_t = x_d.rearrange("(t p) d -> p t d", p=P)
            sp.dma_start(x[:, 0, :], x_t[:, 0, :]).then_inc(s_xin[0], 16)
            sp.dma_start(small[:, :, :], small_d).then_inc(s_const, 16)
            sp.dma_start(cc[:, :], consts_d).then_inc(s_const, 16)
            sp.dma_start(x[:, 1, :], x_t[:, 1, :]).then_inc(s_xin[1], 16)

            def load_w(n):
                m, b = divmod(n, WBLOCKS)
                if n >= WS:
                    pm, pb = divmod(n - WS, WBLOCKS)
                    ready(sp, pm, W_JOB[pb])
                sp.dma_start(w[:, n % WS, :, :], wall_d[m // 2, b]).then_inc(s_w[n % WS], 16)

            for n in range(WS):
                load_w(n)
            sp.dma_start(late[:, :, :], late_d[0]).then_inc(s_late, 16)
            sp.dma_start(g2b[:, :], g2b_d[0]).then_inc(s_g2b, 16)
            sp.dma_start(x[:, TT:, :], x_t[:, TT:, :]).then_inc(s_xrest, 16)
            for n in range(WS, NBLK * WBLOCKS):
                load_w(n)
                m, b = divmod(n, WBLOCKS)
                if m and m % 2 == 0 and b == WS:
                    ready(sp, m - 1, ("sk", 1, HEADS - 1))
                    sp.dma_start(late[:, :, :], late_d[m // 2]).then_inc(s_late, 16)
                if m and m % 2 == 0 and b == NZ + NV + 12:
                    sp.wait_ge(s_h, (m - 1) * CHUNKS + CHUNKS // 2 + 1)
                    sp.dma_start(g2b[:, :], g2b_d[m // 2]).then_inc(s_g2b, 16)
            first = SEQ // P * (DEPTH - 1)
            for t in range(SEQ // P):
                sp.wait_ge(s_x, first + t + 1)
                sp.dma_start(out_d[t * P:(t + 1) * P, :], x[:, t, :]).then_inc(s_out, 16)
            sp.wait_ge(s_out, 16 * (SEQ // P))

        @block.gpsimd
        def _(pool):
            for m in range(NBLK):
                for head in range(TT * HEADS):
                    g = m * TT * HEADS + head
                    pool.wait_ge(s_idx, g + 1)
                    for k in range(TOPK):
                        n = g * TOPK + k
                        if n >= SLOTS:
                            pool.wait_ge(s_yc, n - SLOTS + 1)
                        pool.indirect_dma_start(
                            gather[:, n % SLOTS, :], None, uv_d[m // 2],
                            bass.IndirectOffsetOnAxis(ap=idx[:, g % 2, k:k + 1], axis=0)
                        ).then_inc(s_g[n % SLOTS], 16)

        def mixer_pe(pe, m):
            layer, half = divmod(m, 2)
            t0 = half * TT

            def start(name):
                n = m * NJOBS + JOB_AT[half][name]
                if n >= BANKS:
                    pm, pj = divmod(n - BANKS, NJOBS)
                    done(pe, pm, JOBS[pm % 2][pj][0])
                return bank_of(m, name)

            def weights(b):
                n = m * WBLOCKS + b
                pe.wait_ge(s_w[n % WS], 16 * (n // WS + 1))
                return w[:, n % WS, :, :]

            def transposes(kind, which):
                yield
                for t in range(TT):
                    pe.wait_ge(s_xn, 4 * m + which + t + 1)
                    for h in range(2):
                        ps = start((kind, t, h))
                        for k in range(4):
                            d = 4 * h + k
                            mm = nc.tensor.transpose(ps[:, k * P:(k + 1) * P], xn[:, t, d * P:(d + 1) * P], ident)
                        mm.then_inc(s_ready, 1)
                    yield

            def project(name, b):
                wt = weights(b)
                ps = start(name)
                for d in range(KD):
                    mm = nc.tensor.matmul(ps[:, 0:HALF], wt[:, d, :], xnT[:, d, :], start=d == 0, stop=d == KD - 1)
                mm.then_inc(s_ready, 1)

            if m == 0:
                pe.wait_ge(s_const, CONSTS)
            yield from transposes("xT", 0)
            done(pe, m, ("xT", TT - 1, 1))
            for i in range(NORMED + NV):
                if i < NORMED:
                    project(("z", i), i)
                else:
                    wt = weights(i)
                    ps = start(("v", i - NORMED))
                    for t in range(TT):
                        for d in range(KD):
                            mm = nc.tensor.matmul(ps[:, t * P:(t + 1) * P], xnT[:, d, t * P:(t + 1) * P], wt[:, d, :],
                                                  start=d == 0, stop=d == KD - 1)
                    mm.then_inc(s_ready, 1)
                if 0 < i <= NORMED:
                    ps = start(("n", i - 1))
                    pe.wait_ge(s_sq, 15 * m + i)
                    nc.tensor.matmul(ps[:, 0:HALF], ones64 if i - 1 <= ZKB else ones32, sq[:, (15 * m + i - 1) % 2, :],
                                     start=True, stop=True).then_inc(s_ready, 1)
                yield
            ahead = AHEAD[half]
            at, ptb = sc[half], pt[half]

            def sum_squares(n):
                ps = start(("y", n))
                pe.wait_ge(s_sq, 15 * m + NORMED + n + 1)
                nc.tensor.matmul(ps[:, 0:HALF], ones64, sq[:, (15 * m + NORMED + n) % 2, :], start=True, stop=True)\
                    .then_inc(s_ready, 1)

            def attn_scores(a):
                swa, t, h, k0 = item(a, t0)
                tq, keys = (t - t0) * P, slice(k0 * P, (t + 1) * P)
                for mp in range(1 if swa else 2):
                    ps = start(("s", a, mp))
                    if swa:
                        rows = slice(64 * (h // 2), 64 * (h // 2) + 64)
                        q, k = zt[rows, h % 2, tq:tq + P], kB[rows, keys]
                    else:
                        row = 64 * (h % 2) + 32 * mp
                        rows = slice(row, row + 32)
                        q, k = zt[rows, 2 + h // 2, tq:tq + P], kD[rows, h // 2, keys]
                    nc.tensor.matmul(ps[:, 0:(t + 1 - k0) * P], q, k, start=True, stop=True).then_inc(s_ready, 1)

            pe.wait_ge(s_nrm, 15 * m + NORMED)
            for a in range(ahead):
                attn_scores(a)
            yield
            for a in range(ITEMS + 1):
                if a < ITEMS:
                    swa, t, h, k0 = item(a, t0)
                    ps = start(("t", a))
                    pe.wait_ge(s_pw, ITEMS * m + a + 1)
                    for b in range(t + 1 - k0):
                        mm = nc.tensor.transpose(ps[:, b * P:(b + 1) * P], at[:, a % ahead, 0, b * P:(b + 1) * P], ident)
                    mm.then_inc(s_ready, 1)
                    if a + ahead < ITEMS:
                        attn_scores(a + ahead)
                if a:
                    swa, t, h, k0 = item(a - 1, t0)
                    ps = start(("o", a - 1))
                    done(pe, m, ("t", a - 1))
                    col = (h // 2) * 64 if swa else P + h * 64
                    rows = slice(64 * (h % 2), 64 * (h % 2) + 64)
                    n = t + 1 - k0
                    for b in range(n):
                        mm = nc.tensor.matmul(ps[rows, 0:P], vAll[:, k0 + b, col:col + 64],
                                              ptb[:, (a - 1) % ahead, b * P:(b + 1) * P], start=b == 0, stop=b == n - 1)
                    mm.then_inc(s_ready, 1)
                if a < NZ - NORMED:
                    project(("z", NORMED + a), NV + NORMED + a)
                if a == POOL_AT:
                    pe.wait_ge(s_late, 16 * (layer + 1))
                    for j in range(2):
                        ps = start(("pool", j))
                        pe.wait_ge(s_pd, 2 * m + j + 1)
                        nc.tensor.matmul(ps[:, 0:HALF], wpool[:, j, :], pd[:, j, :], start=True, stop=True)\
                            .then_inc(s_ready, 1)
                if a > POOL_AT:
                    sum_squares(a - POOL_AT - 1)
                yield
            for n in range(ITEMS - POOL_AT, 8):
                sum_squares(n)
                yield
            pe.wait_ge(s_nrm, 15 * m + 13)
            for i in range(8):
                wt = weights(NZ + NV + i)
                ps = start(("out", i))
                for t in range(TT):
                    for n, c in enumerate(YORDER):
                        if i == t == 0 and n == 6:
                            pe.wait_ge(s_nrm, 15 * m + 15)
                        mm = nc.tensor.matmul(ps[:, t * P:(t + 1) * P], yT[:, c, t * P:(t + 1) * P], wt[:, c, :],
                                              start=n == 0, stop=n == 7)
                mm.then_inc(s_ready, 1)
                yield
            yield from transposes("x2T", 2)
            done(pe, m, ("x2T", TT - 1, 1))
            def key_scores(t, h):
                ps = start(("sk", t, h))
                done(pe, m, ("q", 2 * h + 1))
                for k in range(2):
                    hc = 2 * h + k
                    mm = nc.tensor.matmul(ps[:, k * P:(k + 1) * P], qT[:, hc, t * P:(t + 1) * P],
                                          skt[:, k, :], start=True, stop=True)
                mm.then_inc(s_ready, 1)

            for i in range(16):
                project(("q", i), NZ + NV + 8 + i)
                yield
                if i % 2:
                    key_scores(0, i // 2)
                    yield
            for h in range(HEADS):
                key_scores(1, h)
                if h % 2:
                    yield

        def chunk_pe(pe, c):
            for j in range(CH):
                n = c * CH + j
                k = n % (HEADS * TOPK)
                if k == 0 and n:
                    pe.wait_ge(s_x, n // (HEADS * TOPK))
                pe.wait_ge(s_dg, n + 1)
                for hf in range(2):
                    mm = nc.tensor.matmul(ysum[:, hf * 512:(hf + 1) * 512], diag[:, n % NDIAG, :],
                                          gather[:, n % SLOTS, DM + hf * 512:DM + (hf + 1) * 512],
                                          start=k == 0, stop=k == HEADS * TOPK - 1)
                mm.then_inc(s_yc, 1)

        def peer_pe(pe, m):
            for c in range(CHUNKS):
                chunk_pe(pe, m * CHUNKS + c)
                yield

        @block.tensor
        def _(pe):
            first = head_start(mixer_pe(pe, 0))
            for m in range(NBLK):
                interleave(m, lambda n: mixer_pe(pe, n), peer_pe(pe, m), first, slices_first=True)

        def mixer_act(act, m):
            layer, half = divmod(m, 2)
            t0 = half * TT
            mean = 1.0 / DM

            def x_rms(which):
                for t in range(TT):
                    if m == 0 and which == 0:
                        act.wait_ge(s_xin[t], 16)
                    nc.scalar.activation(xn[:, t, :], x[:, t0 + t, :], ACT.Square, accum_out=ss[:, which + t:which + t + 1])\
                        .then_inc(s_actc, 1)
                    actc[0] += 1
                    act.wait_ge(s_actc, actc[0])
                    nc.scalar.activation(sdv[:, which + t:which + t + 1], ss[:, which + t:which + t + 1], ACT.Sqrt,
                                         bias=eps, scale=mean).then_inc(s_sd, 1)
                for _ in range(TT + 1):
                    yield

            def square(n, src):
                nn = 15 * m + n
                if nn >= 2:
                    pm, pn = divmod(nn - 2, 15)
                    ready(act, pm, ("n", pn) if pn < NORMED else ("y", pn - NORMED))
                nc.scalar.activation(sq[:, nn % 2, :], src, ACT.Square).then_inc(s_sq, 1)

            def root(name, n, width):
                nn = 15 * m + n
                ready(act, m, name)
                if nn >= 2:
                    act.wait_ge(s_nrm, nn - 1)
                nc.scalar.activation(sd[:, nn % 2, :], bank_of(m, name)[:, 0:HALF], ACT.Sqrt, bias=eps,
                                     scale=1.0 / width).then_inc(s_done["act"], 1)

            def empty(name, out, in_):
                ready(act, m, name)
                nc.scalar.activation(out, in_, ACT.Copy).then_inc(s_done["act"], 1)

            if m == 0:
                act.wait_ge(s_const, CONSTS)
            elif m == 1:
                act.wait_ge(s_xrest, 16)
            elif layer:
                act.wait_ge(s_x, 2 * m - 2)
            if m:
                ready(act, m - 1, ("x2T", TT - 1, 1))
            yield from x_rms(0)
            for i in range(NORMED + NV):
                if i < NORMED:
                    empty(("z", i), z_home(i, half), bank_of(m, ("z", i))[:, 0:HALF])
                    done(act, m, ("z", i))
                    square(i, z_home(i, half))
                else:
                    empty(("v", i - NORMED), vAll[:, t0:t0 + TT, (i - NORMED) * P:(i - NORMED + 1) * P],
                          bank_of(m, ("v", i - NORMED))[:, 0:HALF].rearrange("p (t c) -> p t c", t=TT))
                if 0 < i <= NORMED:
                    root(("n", i - 1), i - 1, 64 if i - 1 <= ZKB else 32)
                yield
            ahead = AHEAD[half]
            at, ptb = sc[half], pt[half]

            complete = {0: lambda: act.wait_ge(s_cv, 2 * m + 1), 1: lambda: act.wait_ge(s_cv, 2 * m + 2),
                        2: lambda: done(act, m, ("pool", 1)), 4: lambda: done(act, m, ("o", 7)),
                        6: lambda: done(act, m, ("o", 13)), 7: lambda: done(act, m, ("o", 15))}

            def square_y(n):
                if n in complete:
                    complete[n]()
                square(NORMED + n, yT[:, YORDER[n], :])

            def attn_exp(a):
                swa, t, h, k0 = item(a, t0)
                s, cols = a % ahead, (t + 1 - k0) * P
                act.wait_ge(s_nb, ITEMS * m + a + 1)
                scale = (64 ** -0.5) * slope(h) if swa else (32 ** -0.5) * slope(4 + h)
                for mp in range(1 if swa else 2):
                    e = nc.scalar.activation(at[:, s, mp, 0:cols], at[:, s, mp, 0:cols], ACT.Exp,
                                             bias=st[:, s, 2 + mp:3 + mp], scale=scale,
                                             accum_out=st[:, s, 4 + mp:5 + mp])
                if swa:
                    e = nc.scalar.activation(st[:, s, 6:7], small[:, layer, SP_SINK + h:SP_SINK + h + 1], ACT.Exp,
                                             bias=st[:, s, 2:3])
                e.then_inc(s_ex, 1)

            for a in range(ahead - 1 + half):
                attn_exp(a)
            if m == 0:
                act.wait_ge(s_prep, 2)
            yield
            for a in range(ITEMS + 1):
                if a < ITEMS:
                    swa, t, h, k0 = item(a, t0)
                    cols = (t + 1 - k0) * P
                    if half == 0 and a + ahead - 1 < ITEMS:
                        attn_exp(a + ahead - 1)
                    ready(act, m, ("t", a))
                    nc.scalar.activation(ptb[:, a % ahead, 0:cols], bank_of(m, ("t", a))[:, 0:cols], ACT.Copy)\
                        .then_inc(s_done["act"], 1)
                if a:
                    swa, t, h, k0 = item(a - 1, t0)
                    rows = slice(64 * (h % 2), 64 * (h % 2) + 64)
                    empty(("o", a - 1), yT[rows, (2 if swa else 6) + h // 2, (t - t0) * P:(t - t0 + 1) * P],
                          bank_of(m, ("o", a - 1))[rows, 0:P])
                if a < NZ - NORMED:
                    i = NORMED + a
                    empty(("z", i), z_home(i, half), bank_of(m, ("z", i))[:, 0:HALF])
                if a == POOL_AT:
                    for j in range(2):
                        empty(("pool", j), yT[:, j, :], bank_of(m, ("pool", j))[:, 0:HALF])
                if a > POOL_AT:
                    root(("y", a - POOL_AT - 1), NORMED + a - POOL_AT - 1, 64)
                if a >= POOL_AT:
                    square_y(a - POOL_AT)
                if half and a + ahead < ITEMS:
                    attn_exp(a + ahead)
                yield
            for n in range(ITEMS - POOL_AT, 8):
                if n + 1 < 8:
                    square_y(n + 1)
                root(("y", n), NORMED + n, 64)
                yield
            for i in range(8):
                yield
            done(act, m, ("out", 7))
            yield from x_rms(2)
            def key_scores(t, h):
                if m:
                    act.wait_ge(s_idx, TT * HEADS * (m - 1) + HEADS * t + h + 1)
                empty(("sk", t, h), scores[:, t, 2 * h:2 * h + 2, :],
                      bank_of(m, ("sk", t, h))[:, 0:2 * NKEYS].rearrange("p (c k) -> p c k", c=2))

            for i in range(16):
                empty(("q", i), qT[:, i, :], bank_of(m, ("q", i))[:, 0:HALF])
                yield
                if i % 2:
                    key_scores(0, i // 2)
                    yield
            for h in range(HEADS):
                key_scores(1, h)
                if h % 2:
                    yield

        def gate_exp(act, g):
            act.wait_ge(s_gm, g + 1)
            nc.scalar.activation(gate_e[:, :], best_v[:, :], ACT.Exp, bias=neg_best[:, :],
                                 accum_out=gate_s[:, 0:1]).then_inc(s_ge, 1)

        def last_diagonals(act, c):
            for j in range(CH):
                n, k = c * CH + j, c % 4 * CH + j
                act.wait_ge(s_hlast, j + 1)
                nc.scalar.activation(gel[:, c % 2, j:j + 1], hdot[:, c % 2, j:j + 1], ACT.Gelu).then_inc(s_gl, 1)
                act.wait_ge(s_gl, c + j + 1)
                nc.scalar.activation(amp[:, c % 2, j:j + 1], gel[:, c % 2, j:j + 1], ACT.Copy,
                                     scale=gate[:, c // 4 % 2, k:k + 1]).then_inc(s_a, 1)
                act.wait_ge(s_a, n + 1)
                act.wait_ge(s_yc, n - NDIAG + 1)
                nc.scalar.activation(diag[:, n % NDIAG, :], ident, ACT.Copy, scale=amp[:, c % 2, j:j + 1]).then_inc(s_dg, 1)

        def diagonals(act, c):
            act.wait_ge(s_h, c + 1)
            nc.scalar.activation(gel[:, c % 2, :], hdot[:, c % 2, :], ACT.Gelu).then_inc(s_gl, 1)
            act.wait_ge(s_gl, c + 1)
            if c % 4 == 0:
                act.wait_ge(s_gate, c // 4 + 1)
            for j in range(CH):
                k = c % 4 * CH + j
                nc.scalar.activation(amp[:, c % 2, j:j + 1], gel[:, c % 2, j:j + 1], ACT.Copy,
                                     scale=gate[:, c // 4 % 2, k:k + 1]).then_inc(s_a, 1)
            for j in range(CH):
                n = c * CH + j
                act.wait_ge(s_a, n + 1)
                if n >= NDIAG:
                    act.wait_ge(s_yc, n - NDIAG + 1)
                nc.scalar.activation(diag[:, n % NDIAG, :], ident, ACT.Copy, scale=amp[:, c % 2, j:j + 1]).then_inc(s_dg, 1)

        def peer_act(act, m):
            for c in range(CHUNKS):
                if m * CHUNKS + c == NBLK * CHUNKS - 1:
                    last_diagonals(act, m * CHUNKS + c)
                else:
                    diagonals(act, m * CHUNKS + c)
                g = m * TT * HEADS + c // 4 + 1
                if c % 4 == 1 and g < NBLK * TT * HEADS:
                    gate_exp(act, g)
                yield

        actc = [0]
        s_actc = sem("s_actc")

        @block.scalar
        def _(act):
            mixer = mixer_act(act, 0)
            next(mixer)
            act.wait_ge(s_lsum, 1)
            nc.scalar.activation(lam_e[:, :, :], lam_s[:, :, :], ACT.Exp).then_inc(s_lexp, 1)
            first = head_start(mixer, 1)
            gate_exp(act, 0)
            for m in range(NBLK):
                interleave(m, lambda n: mixer_act(act, n), peer_act(act, m), first)

        V = nc.vector
        chained = [0]

        def chain(dve, ins):
            chained[0] += 1
            ins.then_inc(s_chain, 1)
            dve.wait_ge(s_chain, chained[0])

        def mixer_dve(dve, m):
            layer, half = divmod(m, 2)
            t0 = half * TT

            def normalise_x(which, kind, gain, rr):
                for t in range(TT):
                    dve.wait_ge(s_sd, 4 * m + which + t + 1)
                    chain(dve, V.reciprocal(rr[t], sdv[:, which + t:which + t + 1]))
                    V.tensor_scalar(xn[:, t, :], x[:, t0 + t, :], rr[t], None, ALU.mult).then_inc(s_xn, 1)
                yield
                for t in range(TT):
                    for h in range(2):
                        ready(dve, m, (kind, t, h))
                        V.tensor_tensor(
                            xnT[:, 4 * h:4 * h + 4, t * P:(t + 1) * P],
                            bank_of(m, (kind, t, h))[:, :].rearrange("p (k c) -> p k c", k=4),
                            small[:, layer, gain + 4 * h:gain + 4 * h + 4].unsqueeze(2).to_broadcast([P, 4, P]),
                            ALU.mult).then_inc(s_done["dve"], 1)
                    yield

            def normalise(n, tile, gain):
                nn = 15 * m + n
                done(dve, m, ("n", n) if n < NORMED else ("y", n - NORMED))
                chain(dve, V.reciprocal(sd[:, nn % 2, :], sd[:, nn % 2, :]))
                V.scalar_tensor_tensor(tile, tile, gain, sd[:, nn % 2, :], ALU.mult, ALU.mult).then_inc(s_nrm, 1)

            if m == 0:
                for t in range(TT):
                    dve.wait_ge(s_xin[t], 16)
            elif m == 1:
                dve.wait_ge(s_xrest, 16)
            elif layer:
                dve.wait_ge(s_x, 2 * m - 2)
            yield from normalise_x(0, "xT", SP_G1, [r1[:, t:t + 1] for t in range(TT)])
            for i in range(NORMED + NV):
                if 0 < i <= NORMED:
                    normalise(i - 1, z_home(i - 1, half), zcol(layer, SP_QKG + i - 1))
                yield

            ahead = AHEAD[half]
            at = sc[half]

            def attn_bias(a):
                swa, t, h, k0 = item(a, t0)
                s, cols = a % ahead, (t + 1 - k0) * P
                scale = (64 ** -0.5) * slope(h) if swa else (32 ** -0.5) * slope(4 + h)
                for mp in range(1 if swa else 2):
                    ready(dve, m, ("s", a, mp))
                    bias = cc[:, CC_DB + 256 - cols:CC_DB + 256] if swa else cc[:, CC_DD + 512 - cols:CC_DD + 512]
                    V.tensor_tensor_reduce(out=at[:, s, mp, 0:cols], in0=bank_of(m, ("s", a, mp))[:, 0:cols], in1=bias,
                                           scale=1.0, scalar=-BIG, op0=ALU.add, op1=ALU.max,
                                           accum_out=st[:, s, mp:mp + 1]).then_inc(s_done["dve"], 1)
                done(dve, m, ("s", a, 0 if swa else 1))
                if swa:
                    chain(dve, V.tensor_scalar(st[:, s, 0:1], st[:, s, 0:1], scale, None, ALU.mult))
                    chain(dve, V.tensor_tensor(st[:, s, 0:1], st[:, s, 0:1],
                                               small[:, layer, SP_SINK + h:SP_SINK + h + 1], ALU.max))
                    V.tensor_scalar(st[:, s, 2:3], st[:, s, 0:1], -1.0, None, ALU.mult).then_inc(s_nb, 1)
                else:
                    V.tensor_scalar(st[:, s, 2:4], st[:, s, 0:2], -scale, None, ALU.mult).then_inc(s_nb, 1)

            def attn_weights(a):
                swa, t, h, k0 = item(a, t0)
                s, cols = a % ahead, (t + 1 - k0) * P
                dve.wait_ge(s_ex, ITEMS * m + a + 1)
                if swa:
                    chain(dve, V.tensor_tensor(st[:, s, 7:8], st[:, s, 4:5], st[:, s, 6:7], ALU.add))
                    chain(dve, V.reciprocal(st[:, s, 8:9], st[:, s, 7:8]))
                    V.tensor_scalar(at[:, s, 0, 0:cols], at[:, s, 0, 0:cols], st[:, s, 8:9], None, ALU.mult)\
                        .then_inc(s_pw, 1)
                else:
                    chain(dve, V.reciprocal(st[:, s, 8:10], st[:, s, 4:6]))
                    chain(dve, V.tensor_tensor(st[:, s, 10:11], st[:, s, 9:10], neg_lam[:, layer:layer + 1], ALU.mult))
                    chain(dve, V.tensor_scalar(at[:, s, 0, 0:cols], at[:, s, 0, 0:cols], st[:, s, 8:9], None, ALU.mult))
                    V.scalar_tensor_tensor(at[:, s, 0, 0:cols], at[:, s, 1, 0:cols], st[:, s, 10:11],
                                           at[:, s, 0, 0:cols], ALU.mult, ALU.add).then_inc(s_pw, 1)

            c0 = half * HALF

            def pool_tile(j):
                done(dve, m, ("z", ZP[j]))
                src = pT[:, j, c0:c0 + PAD + HALF]
                for lv in range(2 + 2 * j):
                    sh = 1 << lv
                    lo = 2 * sh - 1
                    dst = pool_sum[:, lv % 2, :]
                    chain(dve, V.tensor_tensor(dst[:, lo:PAD + HALF], src[:, lo:PAD + HALF],
                                               src[:, lo - sh:PAD + HALF - sh], ALU.add))
                    src = dst
                    part = lv - 2 * j
                    if part < 0:
                        continue
                    rows = slice(64 * part, 64 * part + 64)
                    if half == 0:
                        chain(dve, V.tensor_tensor(pd[rows, j, 0:PAD], dst[rows, PAD:2 * PAD],
                                                   cc[rows, CC_CORR + PAD * j:CC_CORR + PAD * (j + 1)], ALU.mult))
                        chain(dve, V.scalar_tensor_tensor(
                            pd[rows, j, 0:PAD], pd[rows, j, 0:PAD], cc[rows, CC_INVW + j:CC_INVW + j + 1],
                            pT[rows, j, PAD + c0:PAD + c0 + PAD], ALU.mult, ALU.subtract))
                    first = PAD if half == 0 else 0
                    e = V.scalar_tensor_tensor(pd[rows, j, first:HALF], dst[rows, PAD + first:PAD + HALF],
                                               cc[rows, CC_INVW + j:CC_INVW + j + 1],
                                               pT[rows, j, PAD + c0 + first:PAD + c0 + HALF], ALU.mult, ALU.subtract)
                    if part:
                        e.then_inc(s_pd, 1)
                        dve.wait_ge(s_pd, 2 * m + j + 1)
                    else:
                        chain(dve, e)

            def conv_tile(j):
                done(dve, m, ("z", ZC[j]))
                hh, gg, cg = (z_home(z[j], half) for z in (ZH, ZG, ZC))
                yc = yT[:, 4 + j, :]
                chain(dve, V.tensor_tensor(cT[:, j, PAD + c0:PAD + c0 + HALF], cg, hh, ALU.mult))
                tap = [cT[:, j, PAD + c0 - 2 + k:PAD + c0 - 2 + k + HALF] for k in range(3)]
                wc = [zcol(layer, SP_CONV + 2 * k + j) for k in range(3)]
                chain(dve, V.tensor_scalar(yc, tap[0], wc[0], None, ALU.mult))
                chain(dve, V.scalar_tensor_tensor(yc, tap[1], wc[1], yc, ALU.mult, ALU.add))
                chain(dve, V.scalar_tensor_tensor(yc, tap[2], wc[2], yc, ALU.mult, ALU.add))
                V.tensor_tensor(yc, yc, gg, ALU.mult).then_inc(s_cv, 1)

            def normalise_y(n):
                normalise(NORMED + n, yT[:, YORDER[n], :], zcol(layer, SP_OG + YORDER[n]))

            for a in range(ahead):
                attn_bias(a)
            attn_weights(0)
            yield
            for a in range(ITEMS + 1):
                if half == 0 and a + 1 < ITEMS:
                    attn_weights(a + 1)
                if a + ahead < ITEMS:
                    ready(dve, m, ("t", a))
                    attn_bias(a + ahead)
                if a in MEANS_AT:
                    pool_tile(MEANS_AT.index(a))
                if a in CONV_AT:
                    conv_tile(CONV_AT.index(a))
                if half and a + 1 < ITEMS:
                    attn_weights(a + 1)
                if a > POOL_AT:
                    normalise_y(a - POOL_AT - 1)
                yield
            for n in range(ITEMS - POOL_AT, 8):
                normalise_y(n)
                yield
            for i in range(8):
                ready(dve, m, ("out", i))
                V.tensor_tensor(x[:, t0:t0 + TT, i * P:(i + 1) * P],
                                bank_of(m, ("out", i))[:, 0:HALF].rearrange("p (t c) -> p t c", t=TT),
                                x[:, t0:t0 + TT, i * P:(i + 1) * P], ALU.add).then_inc(s_done["dve"], 1)
                yield
            done(dve, m, ("out", 7))
            yield from normalise_x(2, "x2T", SP_G2, [r2[:, t0 + t:t0 + t + 1] for t in range(TT)])
            for i in range(3 * HEADS + 4):
                yield

        def top16(dve, vals, spare, tv, ti):
            chain(dve, V.max(tv[:, 0:8], vals))
            V.max_index(ti[:, 0:8], tv[:, 0:8], vals)
            chain(dve, V.match_replace(spare, tv[:, 0:8], vals, -BIG))
            chain(dve, V.max(tv[:, 8:16], spare))
            chain(dve, V.max_index(ti[:, 8:16], tv[:, 8:16], spare))

        def route_keys(dve, m, head):
            t, h = divmod(head, HEADS)
            done(dve, m, ("sk", t, h))
            for c in range(2):
                top16(dve, scores[:, t, 2 * h + c, :], sc2[:, c, :], top_v[:, c, :], top_i[:, c, :])
            V.tensor_copy(top_f[:, :, :], top_i[:, :, :])
            chain(dve, V.tensor_tensor(cand[:, :, :], top_v[:, 0, :].unsqueeze(2).to_broadcast([P, TOPK, TOPK]),
                                       top_v[:, 1, :].unsqueeze(1).to_broadcast([P, TOPK, TOPK]), ALU.add))

        def route_experts(dve, m, head):
            g = m * TT * HEADS + head
            flat = lambda c: c[:, :, :].rearrange("p a b -> p (a b)")
            if g:
                dve.wait_ge(s_ge, g)
            top16(dve, flat(cand), flat(cand2), best_v, best_p)
            V.tensor_scalar(neg_best[:, :], best_v[:, 0:1], -1.0, None, ALU.mult).then_inc(s_gm, 1)
            V.tensor_scalar(pos_u[:, 0, :], best_p[:, :], 4, None, ALU.logical_shift_right)
            chain(dve, V.tensor_scalar(pos_u[:, 1, :], best_p[:, :], 15, None, ALU.bitwise_and))
            chain(dve, V.tensor_copy(pos_f[:, :, :], pos_u[:, :, :]))
            both = [P, 2 * TOPK, TOPK]
            chain(dve, V.tensor_tensor(
                hot[:, :, :], pos_f[:, :, :].rearrange("p c k -> p (c k)").unsqueeze(2).to_broadcast(both),
                cc[:, CC_IOTA:CC_IOTA + TOPK].unsqueeze(1).to_broadcast(both), ALU.is_equal))
            hot4 = hot[:, :, :].rearrange("p (c k) a -> p c k a", c=2)
            chain(dve, V.tensor_tensor(hot4, hot4, top_f[:, :, :].unsqueeze(2).to_broadcast([P, 2, TOPK, TOPK]), ALU.mult))
            chain(dve, V.tensor_reduce(ij[:, :, :].rearrange("p c k -> p (c k)"), hot[:, :, :], AX, ALU.add))
            V.scalar_tensor_tensor(idx[:, g % 2, :], ij[:, 0, :], float(NKEYS), ij[:, 1, :], ALU.mult, ALU.add)\
                .then_inc(s_idx, 1)

        def route_gate(dve, m, head):
            g = m * TT * HEADS + head
            dve.wait_ge(s_ge, g + 1)
            if g >= 2:
                dve.wait_ge(s_a, (g - 1) * TOPK)
            chain(dve, V.reciprocal(gate_s[:, 1:2], gate_s[:, 0:1]))
            V.tensor_scalar(gate[:, g % 2, :], gate_e[:, :], gate_s[:, 1:2], None, ALU.mult).then_inc(s_gate, 1)

        def peer_dve(dve, m):
            layer = m // 2
            def add_tile(tg):
                dve.wait_ge(s_yc, (tg + 1) * HEADS * TOPK)
                t = tg % (SEQ // P)
                V.tensor_tensor(x[:, t, :], ysum[:, :], x[:, t, :], ALU.add).then_inc(s_x, 1)

            per_tile = CHUNKS // TT
            for c in range(CHUNKS):
                cg = m * CHUNKS + c
                t = (m % 2) * TT + c // per_tile
                head = c // 4
                if c % per_tile == 0:
                    if c == 0:
                        done(dve, m, ("out", 7))
                        dve.wait_ge(s_g2b, 16 * (layer + 1))
                    chain(dve, V.scalar_tensor_tensor(xc[:, :], x[:, t, :], r2[:, t:t + 1], g2b[:, :],
                                                      ALU.mult, ALU.mult))
                if cg >= 2:
                    dve.wait_ge(s_gl, cg - 1)
                for j in range(CH):
                    n = cg * CH + j
                    dve.wait_ge(s_g[n % SLOTS], 16 * (n // SLOTS + 1))
                    e = V.tensor_tensor_reduce(out=gather[:, n % SLOTS, 0:DM], in0=gather[:, n % SLOTS, 0:DM],
                                               in1=xc[:, :], scale=1.0, scalar=0.0, op0=ALU.mult, op1=ALU.add,
                                               accum_out=hdot[:, cg % 2, j:j + 1])
                    if cg == NBLK * CHUNKS - 1:
                        e.then_inc(s_hlast, 1)
                    elif j == CH - 1:
                        e.then_inc(s_h, 1)
                if c % per_tile == 0 and cg:
                    add_tile(cg // per_tile - 1)
                nm, nh = divmod(m * TT * HEADS + head + 1, TT * HEADS)
                if nm < NBLK:
                    if c % 4 == 0:
                        route_keys(dve, nm, nh)
                    elif c % 4 == 1:
                        route_experts(dve, nm, nh)
                    elif c % 4 == 3:
                        route_gate(dve, nm, nh)
                yield
            if m == NBLK - 1:
                add_tile(m * TT + 1)

        @block.vector
        def _(dve):
            V.memset(pT[:, :, 0:PAD], 0.0).then_inc(s_prep, 1)
            V.memset(cT[:, :, 0:PAD], 0.0).then_inc(s_prep, 1)
            dve.wait_ge(s_const, CONSTS)
            for layer in range(DEPTH):
                lam = small[:, layer, SP_LAM:SP_LAM + 128].rearrange("p (a b k) -> p a b k", a=2, b=2)
                chain(dve, V.tensor_tensor(lam_t[:, layer, :, :], lam[:, :, 0, :], lam[:, :, 1, :], ALU.mult))
            V.tensor_reduce(lam_s[:, :, :], lam_t[:, :, :, :], AX, ALU.add).then_inc(s_lsum, 1)
            mixer = mixer_dve(dve, 0)
            for _ in range(3):
                next(mixer)
            for layer in range(DEPTH):
                for n, i in enumerate(ZQB + ZQD):
                    gcol = zcol(layer, SP_QKG + i)
                    chain(dve, V.tensor_tensor(gcol, gcol, cc[:, CC_SLI + n:CC_SLI + n + 1], ALU.mult))
                og = small[:, layer, SP_OG + 6:SP_OG + 8]
                chain(dve, V.tensor_scalar(og, og, 1.0 - lam_init(layer), None, ALU.mult))
            dve.wait_ge(s_lexp, 1)
            for layer in range(DEPTH):
                chain(dve, V.tensor_tensor(neg_lam[:, layer:layer + 1], lam_e[:, layer, 1:2], lam_e[:, layer, 0:1],
                                           ALU.subtract))
                chain(dve, V.tensor_scalar(neg_lam[:, layer:layer + 1], neg_lam[:, layer:layer + 1],
                                           -lam_init(layer), None, ALU.add))
            first = head_start(mixer, 3)
            route_keys(dve, 0, 0)
            route_experts(dve, 0, 0)
            route_gate(dve, 0, 0)
            for m in range(NBLK):
                interleave(m, lambda n: mixer_dve(dve, n), peer_dve(dve, m), first)



def columns():
    a, qb, kb, vb, h, b, c, qd, kd, vd = np.cumsum([0, 256, 256, 128, 128, 256, 256, 256, 256, 256])
    r = np.arange
    heads = lambda first, hs: np.concatenate([first + 64 * h + r(64) for h in hs])
    tiles = [heads(qb, (0, 2)), heads(qb, (1, 3)), kb + r(128), qd + r(128), qd + 128 + r(128),
             kd + r(128), kd + 128 + r(128), vb + r(128), vd + r(128), vd + 128 + r(128),
             a + r(128), a + 128 + r(128)]
    for j in range(2):
        tiles += [first + 128 * j + r(128) for first in (h, b, c)]
    return np.concatenate(tiles)


def layout_weights(w_in, w_out, w_query):
    both = np.concatenate([w_in[:, :, columns()], w_out, w_query], axis=2)
    tiled = both.reshape(DEPTH, KD, P, WBLOCKS, P)
    return np.ascontiguousarray(tiled.transpose(0, 3, 2, 1, 4))


def layout_small(i):
    out = np.zeros((P, DEPTH, SP_N), np.float32)
    for l in range(DEPTH):
        s = out[:, l]
        s[:, SP_G1:SP_G1 + 8] = i["norm1_g"][l].reshape(8, P).T
        s[:, SP_G2:SP_G2 + 8] = i["norm2_g"][l].reshape(8, P).T
        s[:, SP_OG:SP_OG + 8] = i["out_norm_g"][l].reshape(8, P).T
        for n, name in enumerate(["swa_q_norm"] * 2 + ["swa_k_norm"] + ["diff_q_norm"] * 2 + ["diff_k_norm"] * 2):
            g = i[name][l]
            s[:, SP_QKG + n] = np.tile(g, P // g.size)
        for k in range(3):
            for j in range(2):
                s[:, SP_CONV + 2 * k + j] = i["conv_w"][l, k, j * P:(j + 1) * P]
        s[:, SP_SINK:SP_SINK + 4] = i["swa_sinks"][l][None]
        s[:, SP_LAM:SP_LAM + 128] = np.concatenate([i[n][l] for n in ("lam_q1", "lam_k1", "lam_q2", "lam_k2")])[None]
    return out


def layout_consts():
    c = np.zeros((P, CC_N), np.float32)
    q = np.arange(P)[:, None]
    c[:, CC_ID:CC_ID + P] = np.eye(P)
    c[:, CC_O64:CC_O64 + P] = q // 64 == np.arange(P)[None] // 64
    c[:, CC_O32:CC_O32 + P] = q // 32 == np.arange(P)[None] // 32
    dist = q + 128 - np.arange(256)[None]
    c[:, CC_DB:CC_DB + 256] = np.where((dist >= 0) & (dist < 128), -dist * math.sqrt(64), MASK)
    dist = q + 384 - np.arange(512)[None]
    c[:, CC_DD:CC_DD + 512] = np.where(dist >= 0, -dist * math.sqrt(32), MASK)
    c[:, CC_IOTA:CC_IOTA + TOPK] = np.arange(TOPK)[None]
    for j in range(2):
        for part in range(2):
            win = 2 ** (2 * j + part + 1)
            rows = slice(64 * part, 64 * part + 64)
            c[rows, CC_INVW + j] = 1.0 / win
            c[rows, CC_CORR + PAD * j:CC_CORR + PAD * (j + 1)] = win / np.minimum(np.arange(PAD) + 1, win)
    for rows, base in ((slice(0, 64), 0), (slice(64, 128), 1)):
        for g in range(2):
            c[rows, CC_SLI + g] = 1.0 / slope(2 * base + g)
            c[rows, CC_SLI + 2 + g] = 1.0 / slope(4 + 2 * g + base)
    c[:, CC_EPS] = EPS
    return c


def kernel(**inputs):
    import concourse.bacc as bacc
    from concourse.bass_utils import run_bass_kernel_spmd as run
    i = {k: np.asarray(v) for k, v in inputs.items()}
    wp = np.zeros((P, DEPTH, 2, P), np.float32)
    for l in range(DEPTH):
        for g in range(4):
            r = slice(64 * (g % 2), 64 * (g % 2) + 64)
            wp[r, l, g // 2, r] = i["w_pool"][l, g]
    arrays = {
        "x_in": np.ascontiguousarray(i["x"].reshape(SEQ, DM)),
        "weights": layout_weights(i["w_in"], i["w_out"], i["w_query"]),
        "small_in": layout_small(i),
        "consts_in": layout_consts(),
        "g2_rows": np.ascontiguousarray(np.broadcast_to(i["norm2_g"][:, None, :], (DEPTH, P, DM))),
        "late_in": np.ascontiguousarray(np.concatenate([wp, i["sub_keys"].transpose(3, 0, 1, 2)], axis=2).swapaxes(0, 1)),
    }
    for l in range(DEPTH):
        arrays[f"experts{l}"] = np.concatenate([i["peer_u"][l], i["peer_v"][l]], axis=1)
    nc = bacc.Bacc("TRN2", target_bir_lowering=False, num_devices=1)
    aps = [nc.dram_tensor(n, a.shape, mybir.dt.from_np(a.dtype), kind="ExternalInput").ap() for n, a in arrays.items()]
    out = nc.dram_tensor("y_out", (SEQ, DM), mybir.dt.float32, kind="ExternalOutput").ap()
    build(nc, *aps[:6], aps[6:], out)
    r = run(nc, [arrays], core_ids=[0])
    return r.results[0]["y_out"].reshape(1, SEQ, DM)
```
